# Optimizing a Trainium2 kernel written in Bass

```python
import math
import jax, jax.numpy as jnp
from jax import lax
import numpy as np

D_MODEL = 2048
BATCH = 1
SEQ = 256
DEPTH = 2

GRID_W = 64
CTX_LEN = 256
D_MIX = D_MODEL
D_CONV = D_MIX // 4
D_ATTN = D_MIX // 2
D_POOL = D_MIX // 4
N_HEADS = 8
V_DIM = D_ATTN // N_HEADS
QK_DIM = V_DIM // 2
ATTN_SCALE = QK_DIM ** -0.5
Q_BLOCK = 128
CONV_W = 3
POOL_WINDOWS = (2, 4, 8, 16)
N_POOL_GROUPS = 4
POOL_GROUP = D_POOL // N_POOL_GROUPS
ROPE_THETA = 10000.0
LN_EPS = 1e-5
RMS_EPS = 1e-5
DEEPNORM_ALPHA = (2 * DEPTH) ** 0.25
DEEPNORM_BETA = (8 * DEPTH) ** -0.25
SPLIT_SIZES = (D_CONV, D_CONV, D_CONV, D_CONV, D_ATTN, D_ATTN, D_ATTN, D_ATTN, D_POOL, D_POOL)
SPLIT_POINTS = tuple(int(s) for s in np.cumsum(SPLIT_SIZES)[:-1])
D_IN = sum(SPLIT_SIZES)
ATT_K_OFF = 4 * D_CONV + D_ATTN
ATT_V_END = 4 * D_CONV + 3 * D_ATTN


def _layernorm(x, g, b):
    xf = x.astype(jnp.float32)
    mu = jnp.mean(xf, axis=-1, keepdims=True)
    var = jnp.mean(jnp.square(xf - mu), axis=-1, keepdims=True)
    return ((xf - mu) * lax.rsqrt(var + LN_EPS) * g + b).astype(x.dtype)

def _qk_heads(t):
    return t.reshape(t.shape[0], t.shape[1], N_HEADS, 2, QK_DIM)

def _v_heads(t):
    return t.reshape(t.shape[0], t.shape[1], N_HEADS, V_DIM)

def _rope_axial(x, rows, cols):
    half = QK_DIM // 2
    n = half // 2
    inv = ROPE_THETA ** (-jnp.arange(n, dtype=jnp.float32) / n)

    def rot(v, pos):
        ang = pos.astype(jnp.float32)[:, None] * inv
        cos = jnp.cos(ang)[None, :, None, None, :]
        sin = jnp.sin(ang)[None, :, None, None, :]
        v1, v2 = v[..., :n], v[..., n:]
        return jnp.concatenate([v1 * cos - v2 * sin, v1 * sin + v2 * cos], axis=-1)

    xf = x.astype(jnp.float32)
    return jnp.concatenate([rot(xf[..., :half], rows), rot(xf[..., half:], cols)], axis=-1).astype(x.dtype)

def _diff_attn(qb, k_all, v_all, lam):
    s = jnp.einsum('bqhid,bkhid->bhiqk', qb.astype(jnp.float32) * ATTN_SCALE, k_all.astype(jnp.float32))
    p = jax.nn.softmax(s, axis=-1)
    a = p[:, :, 0] - lam * p[:, :, 1]
    return jnp.einsum('bhqk,bkhe->bqhe', a.astype(v_all.dtype), v_all)

def _diff_subln(o, g, lam_init):
    of = o.astype(jnp.float32)
    y = of * lax.rsqrt(jnp.mean(jnp.square(of), axis=-1, keepdims=True) + RMS_EPS) * g * (1.0 - lam_init)
    return y.reshape(o.shape[0], o.shape[1], D_ATTN).astype(o.dtype)

def _short_conv(u, b_gate, c_gate, g, w):
    v = c_gate * u
    T = u.shape[1]
    vp = jnp.pad(v, ((0, 0), (1, 1), (0, 0)))
    y = vp[:, :T] * w[0] + vp[:, 1:T + 1] * w[1] + vp[:, 2:] * w[2]
    return jax.nn.silu(g) * (b_gate * y)

def _multiscale_pool(u, g, pool_w_l, pool_scale_l):
    B, T, _ = u.shape
    ug = u.reshape(B, T, N_POOL_GROUPS, POOL_GROUP).astype(jnp.float32)
    csum = jnp.concatenate([jnp.zeros_like(ug[:, :1]), jnp.cumsum(ug, axis=1)], axis=1)
    t = jnp.arange(T)
    diffs = []
    for gi, w in enumerate(POOL_WINDOWS):
        lo = jnp.clip(t - w // 2, 0, T)
        hi = jnp.clip(t + w - w // 2, 0, T)
        mean = (csum[:, hi, gi] - csum[:, lo, gi]) / (hi - lo).astype(jnp.float32)[None, :, None]
        diffs.append(mean - ug[:, :, gi])
    d = jnp.stack(diffs, axis=2).astype(u.dtype)
    y = jnp.einsum('btgc,gcd->btgd', d, pool_w_l).reshape(B, T, D_POOL) * pool_scale_l
    return jax.nn.silu(g) * y

def _mix_output(parts, att, lam_init, conv_w_l, subln_g_l, pool_w_l, pool_scale_l, w_out_l):
    cu, cb, cc, cg, _q, _k, _v, ag, pu, pg = parts
    y_conv = _short_conv(cu, cb, cc, cg, conv_w_l)
    y_attn = jax.nn.silu(ag) * _diff_subln(att, subln_g_l, lam_init)
    y_pool = _multiscale_pool(pu, pg, pool_w_l, pool_scale_l)
    return jnp.concatenate([y_conv, y_attn, y_pool], axis=-1) @ w_out_l

def first_inputs(seed: int = 0) -> dict:
    key = jax.random.key(seed)
    ks = jax.random.split(key, 18)
    f32 = jnp.float32

    def nrm(k, shape, s):
        return s * jax.random.normal(k, shape, f32)

    return {
        'x': nrm(ks[0], (BATCH, SEQ, D_MODEL), 1.0),
        'c': nrm(ks[1], (BATCH, D_MODEL), 1.0),
        'ctx': nrm(ks[2], (BATCH, CTX_LEN, D_MODEL), 1.0),
        'c_ctx': nrm(ks[3], (D_MODEL,), 1.0),
        'w_mod': nrm(ks[4], (DEPTH, D_MODEL, 3 * D_MODEL), 0.5 * D_MODEL ** -0.5),
        'b_mod': nrm(ks[5], (DEPTH, 3 * D_MODEL), 0.02),
        'w_in': nrm(ks[6], (DEPTH, D_MODEL, D_IN), D_MODEL ** -0.5),
        'conv_w': nrm(ks[7], (DEPTH, CONV_W, D_CONV), CONV_W ** -0.5),
        'lam_q1': nrm(ks[8], (DEPTH, QK_DIM), 0.1),
        'lam_k1': nrm(ks[9], (DEPTH, QK_DIM), 0.1),
        'lam_q2': nrm(ks[10], (DEPTH, QK_DIM), 0.1),
        'lam_k2': nrm(ks[11], (DEPTH, QK_DIM), 0.1),
        'subln_g': 1.0 + nrm(ks[12], (DEPTH, V_DIM), 0.02),
        'pool_w': nrm(ks[13], (DEPTH, N_POOL_GROUPS, POOL_GROUP, POOL_GROUP), POOL_GROUP ** -0.5),
        'pool_scale': 1.0 + nrm(ks[14], (DEPTH, D_POOL), 0.02),
        'w_out': nrm(ks[15], (DEPTH, D_MIX, D_MODEL), DEEPNORM_BETA * D_MIX ** -0.5),
        'ln_g': 1.0 + nrm(ks[16], (DEPTH, D_MODEL), 0.02),
        'ln_b': nrm(ks[17], (DEPTH, D_MODEL), 0.02),
    }

def first_block(x, c, ctx, c_ctx, w_mod, b_mod, w_in, conv_w, lam_q1, lam_k1, lam_q2, lam_k2,
              subln_g, pool_w, pool_scale, w_out, ln_g, ln_b):
    B, L, _ = x.shape
    ROWS = L // GRID_W
    rows = jnp.repeat(jnp.arange(ROWS, dtype=jnp.int32), GRID_W)
    cols = jnp.broadcast_to(jnp.arange(GRID_W, dtype=jnp.int32)[None, :], (ROWS, GRID_W)).reshape(-1)
    n_blk = L // Q_BLOCK
    xl, xc = x, ctx
    for l in range(DEPTH):
        last = l == DEPTH - 1
        sh_l, sc_l, g_l = jnp.split(jax.nn.silu(c) @ w_mod[l] + b_mod[l], 3, axis=-1)
        sh_c, sc_c, g_c = jnp.split(jax.nn.silu(c_ctx) @ w_mod[l] + b_mod[l], 3, axis=-1)
        hl = xl * (1.0 + sc_l[:, None, :]) + sh_l[:, None, :]
        hc = xc * (1.0 + sc_c) + sh_c
        lam_init = 0.8 - 0.6 * math.exp(-0.3 * l)
        lam = (jnp.exp(jnp.sum(lam_q1[l].astype(jnp.float32) * lam_k1[l].astype(jnp.float32)))
               - jnp.exp(jnp.sum(lam_q2[l].astype(jnp.float32) * lam_k2[l].astype(jnp.float32)))
               + lam_init)
        parts_l = jnp.split(hl @ w_in[l], SPLIT_POINTS, axis=-1)
        ql = _rope_axial(_qk_heads(parts_l[4]), rows, cols)
        kl = _rope_axial(_qk_heads(parts_l[5]), rows, cols)
        vl = _v_heads(parts_l[6])
        if last:
            kc, vc = jnp.split(hc @ w_in[l][:, ATT_K_OFF:ATT_V_END], 2, axis=-1)
            parts_c = None
        else:
            parts_c = jnp.split(hc @ w_in[l], SPLIT_POINTS, axis=-1)
            kc, vc = parts_c[5], parts_c[6]
        kc = _qk_heads(kc)
        vc = _v_heads(vc)
        k_all = jnp.concatenate([kc, kl], axis=1)
        v_all = jnp.concatenate([vc, vl], axis=1)
        q_blocks = ql.reshape(B, n_blk, Q_BLOCK, N_HEADS, 2, QK_DIM).swapaxes(0, 1)
        att_l = lax.map(lambda qb: _diff_attn(qb, k_all, v_all, lam), q_blocks)
        att_l = att_l.swapaxes(0, 1).reshape(B, L, N_HEADS, V_DIM)
        out_l = _mix_output(parts_l, att_l, lam_init, conv_w[l], subln_g[l], pool_w[l], pool_scale[l], w_out[l])
        xl_new = _layernorm(DEEPNORM_ALPHA * xl + g_l[:, None, :] * out_l, ln_g[l], ln_b[l])
        if not last:
            att_c = _diff_attn(_qk_heads(parts_c[4]), kc, vc, lam)
            out_c = _mix_output(parts_c, att_c, lam_init, conv_w[l], subln_g[l], pool_w[l], pool_scale[l], w_out[l])
            xc = _layernorm(DEEPNORM_ALPHA * xc + g_c * out_c, ln_g[l], ln_b[l])
        xl = xl_new
    return xl


DEPTH_2 = 1

HEAD_DIM = 128
N_HEADS_MOBA = D_MODEL // (2 * HEAD_DIM)
N_HEADS_FOX = D_MODEL // (2 * HEAD_DIM)
MOBA_WIDTH = N_HEADS_MOBA * HEAD_DIM
FOX_WIDTH = N_HEADS_FOX * HEAD_DIM
MOBA_BLOCK = 256
MOBA_TOPK = 3
MOBA_Q_CHUNK = 64
FOX_Q_BLOCK = 128
D_FF = 4 * D_MODEL
RMS_EPS_2 = 1e-6
IN_WIDTHS = (MOBA_WIDTH, MOBA_WIDTH, MOBA_WIDTH,
             FOX_WIDTH, FOX_WIDTH, FOX_WIDTH,
             N_HEADS_FOX,
             D_MODEL, D_MODEL)
D_IN_2 = sum(IN_WIDTHS)


def rms_norm(x, g):
    xf = x.astype(jnp.float32)
    y = xf * lax.rsqrt(jnp.mean(xf * xf, axis=-1, keepdims=True) + RMS_EPS_2)
    return (y * g.astype(jnp.float32)).astype(x.dtype)

def split_heads(t, n_heads):
    b, s, _ = t.shape
    return t.reshape(b, s, n_heads, HEAD_DIM).transpose(0, 2, 1, 3)

def merge_heads(t):
    b, h, s, d = t.shape
    return t.transpose(0, 2, 1, 3).reshape(b, s, h * d)

def to_chunks(a, c):
    a = a.reshape(a.shape[:2] + (a.shape[2] // c, c) + a.shape[3:])
    return jnp.moveaxis(a, 2, 0)

def from_chunks(a):
    a = jnp.moveaxis(a, 0, 2)
    return a.reshape(a.shape[:2] + (a.shape[2] * a.shape[3],) + a.shape[4:])

def alibi_slopes(n_heads):
    return jnp.exp2(-8.0 * jnp.arange(1, n_heads + 1, dtype=jnp.float32) / n_heads)

def moba_attention(q, k, v):
    b, h, s, d = q.shape
    s_pad = -(-s // MOBA_BLOCK) * MOBA_BLOCK
    pad = ((0, 0), (0, 0), (0, s_pad - s), (0, 0))
    q, k, v = jnp.pad(q, pad), jnp.pad(k, pad), jnp.pad(v, pad)
    nb = s_pad // MOBA_BLOCK
    n_sel = min(MOBA_TOPK, nb)
    scale = HEAD_DIM ** -0.5
    slopes = alibi_slopes(h)[None, :, None]
    kb = k.reshape(b, h, nb, MOBA_BLOCK, d)
    vb = v.reshape(b, h, nb, MOBA_BLOCK, d)
    kmean = jnp.mean(kb.astype(jnp.float32), axis=3)
    gate = jnp.einsum('bhtd,bhnd->bhtn', q.astype(jnp.float32), kmean)
    q_blk = jnp.arange(s_pad) // MOBA_BLOCK
    past = jnp.arange(nb)[None, :] < q_blk[:, None]
    gate = jnp.where(past, gate, -jnp.inf)
    top_vals, sel = lax.top_k(gate, n_sel)
    valid = jnp.isfinite(top_vals)
    bi = jnp.arange(b)[:, None, None, None]
    hi = jnp.arange(h)[None, :, None, None]
    blk_off = jnp.arange(MOBA_BLOCK)

    def chunk(args):
        ci, qc, selc, validc = args
        q_pos = ci * MOBA_Q_CHUNK + jnp.arange(MOBA_Q_CHUNK)
        own = (ci * MOBA_Q_CHUNK) // MOBA_BLOCK
        k_own = lax.dynamic_index_in_dim(kb, own, axis=2, keepdims=False)
        v_own = lax.dynamic_index_in_dim(vb, own, axis=2, keepdims=False)
        dist_own = (q_pos[:, None] - (own * MOBA_BLOCK + blk_off)[None, :])
        s_own = jnp.einsum('bhcd,bhsd->bhcs', qc, k_own).astype(jnp.float32) * scale
        s_own = s_own - slopes[..., None] * jnp.abs(dist_own).astype(jnp.float32)
        s_own = jnp.where(dist_own >= 0, s_own, -jnp.inf)
        k_sel = kb[bi, hi, selc]
        v_sel = vb[bi, hi, selc]
        s_sel = jnp.einsum('bhcd,bhcjsd->bhcjs', qc, k_sel).astype(jnp.float32) * scale
        sel_pos = selc[..., None] * MOBA_BLOCK + blk_off
        dist_sel = jnp.abs(q_pos[None, None, :, None, None] - sel_pos).astype(jnp.float32)
        s_sel = s_sel - slopes[..., None, None] * dist_sel
        s_sel = jnp.where(validc[..., None], s_sel, -jnp.inf)
        c, j = selc.shape[2], selc.shape[3]
        scores = jnp.concatenate([s_sel.reshape(b, h, c, j * MOBA_BLOCK), s_own], axis=-1)
        p = jax.nn.softmax(scores, axis=-1).astype(v.dtype)
        p_sel = p[..., :j * MOBA_BLOCK].reshape(b, h, c, j, MOBA_BLOCK)
        p_own = p[..., j * MOBA_BLOCK:]
        return (jnp.einsum('bhcjs,bhcjsd->bhcd', p_sel, v_sel)
                + jnp.einsum('bhcs,bhsd->bhcd', p_own, v_own))

    nc = s_pad // MOBA_Q_CHUNK
    out = lax.map(chunk, (jnp.arange(nc), to_chunks(q, MOBA_Q_CHUNK),
                          to_chunks(sel, MOBA_Q_CHUNK), to_chunks(valid, MOBA_Q_CHUNK)))
    return from_chunks(out)[:, :, :s]

def forgetting_attention(q, k, v, f_logit, b_forget):
    b, h, s, d = q.shape
    scale = HEAD_DIM ** -0.5
    log_f = jax.nn.log_sigmoid(f_logit.astype(jnp.float32) + b_forget.astype(jnp.float32))
    c = jnp.cumsum(log_f, axis=1).transpose(0, 2, 1)
    key_pos = jnp.arange(s)

    def chunk(args):
        ci, qc, cq = args
        sc = jnp.einsum('bhcd,bhsd->bhcs', qc, k).astype(jnp.float32) * scale
        sc = sc + cq[..., None] - c[:, :, None, :]
        q_pos = ci * FOX_Q_BLOCK + jnp.arange(FOX_Q_BLOCK)
        sc = jnp.where(q_pos[:, None] >= key_pos[None, :], sc, -jnp.inf)
        p = jax.nn.softmax(sc, axis=-1).astype(v.dtype)
        return jnp.einsum('bhcs,bhsd->bhcd', p, v)

    nc = s // FOX_Q_BLOCK
    cq = c.reshape(b, h, nc, FOX_Q_BLOCK).transpose(2, 0, 1, 3)
    out = lax.map(chunk, (jnp.arange(nc), to_chunks(q, FOX_Q_BLOCK), cq))
    return from_chunks(out)

def second_inputs(seed: int = 0) -> dict:
    key = jax.random.key(seed)
    ks = jax.random.split(key, 11)
    f32 = jnp.float32
    def normal(k, shape, scale):
        return jax.random.normal(k, shape, f32) * scale
    return {
        "x": normal(ks[0], (BATCH, SEQ, D_MODEL), 1.0),
        "norm_mix_g": 1.0 + normal(ks[1], (D_MODEL,), 0.02),
        "w_in": normal(ks[2], (D_MODEL, D_IN_2), D_MODEL ** -0.5),
        "b_forget": 2.0 + normal(ks[3], (N_HEADS_FOX,), 0.5),
        "w_proj_a": normal(ks[4], (MOBA_WIDTH, D_MODEL), MOBA_WIDTH ** -0.5),
        "w_proj_b": normal(ks[5], (FOX_WIDTH, D_MODEL), FOX_WIDTH ** -0.5),
        "w_out": normal(ks[6], (D_MODEL, D_MODEL), D_MODEL ** -0.5),
        "norm_mlp_g": 1.0 + normal(ks[7], (D_MODEL,), 0.02),
        "w_up": normal(ks[8], (D_MODEL, D_FF), D_MODEL ** -0.5),
        "w_down": normal(ks[9], (D_FF, D_MODEL), D_FF ** -0.5),
        "norm_final_g": 1.0 + normal(ks[10], (D_MODEL,), 0.02),
    }

def second_block(x, norm_mix_g, w_in, b_forget, w_proj_a, w_proj_b, w_out,
              norm_mlp_g, w_up, w_down, norm_final_g):
    split_idx = list(np.cumsum(IN_WIDTHS)[:-1])
    for _ in range(DEPTH_2):
        hn = rms_norm(x, norm_mix_g)
        z = hn @ w_in
        q_a, k_a, v_a, q_b, k_b, v_b, f_logit, g_a, g_b = jnp.split(z, split_idx, axis=-1)
        a = moba_attention(split_heads(q_a, N_HEADS_MOBA), split_heads(k_a, N_HEADS_MOBA),
                           split_heads(v_a, N_HEADS_MOBA))
        bfx = forgetting_attention(split_heads(q_b, N_HEADS_FOX), split_heads(k_b, N_HEADS_FOX),
                                   split_heads(v_b, N_HEADS_FOX), f_logit, b_forget)
        a = merge_heads(a) @ w_proj_a
        bfx = merge_heads(bfx) @ w_proj_b
        merged = jax.nn.sigmoid(g_a) * a + jax.nn.sigmoid(g_b) * bfx
        x = x + merged @ w_out
        hm = rms_norm(x, norm_mlp_g)
        x = x + jnp.square(jax.nn.relu(hm @ w_up)) @ w_down
    return rms_norm(x, norm_final_g)


def setup_inputs(seed=0):
    out = dict(first_inputs(seed))
    for name, value in second_inputs(seed + 1).items():
        if name != "x":
            out[name + "_2"] = value
    return out


def reference(
    x, c, ctx, c_ctx, w_mod, b_mod, w_in, conv_w, lam_q1, lam_k1, lam_q2, lam_k2, subln_g,
    pool_w, pool_scale, w_out, ln_g, ln_b, norm_mix_g_2, w_in_2, b_forget_2, w_proj_a_2,
    w_proj_b_2, w_out_2, norm_mlp_g_2, w_up_2, w_down_2, norm_final_g_2,
):
    x = first_block(
        x, c, ctx, c_ctx, w_mod, b_mod, w_in, conv_w, lam_q1, lam_k1, lam_q2, lam_k2, subln_g,
        pool_w, pool_scale, w_out, ln_g, ln_b,
    )
    return second_block(
        x, norm_mix_g_2, w_in_2, b_forget_2, w_proj_a_2, w_proj_b_2, w_out_2, norm_mlp_g_2,
        w_up_2, w_down_2, norm_final_g_2,
    )


_drawn_inputs = setup_inputs


def setup_inputs(seed=0):
    import zlib

    import numpy as np

    out = dict(_drawn_inputs(seed))
    spreads = {}
    factors = {'ctx': 2.933,
     'b_mod': 5.718,
     'lam_q1': 8.0,
     'lam_k1': 8.0,
     'lam_q2': 8.0,
     'lam_k2': 8.0,
     'subln_g': 8.0,
     'pool_scale': 8.0,
     'norm_mix_g_2': 5.645,
     'norm_mlp_g_2': 3.241,
     'norm_final_g_2': 2.764}
    for name, (base, spread) in spreads.items():
        noise = np.random.default_rng([zlib.crc32(name.encode()), seed]).standard_normal(out[name].shape)
        drawn = base * np.exp(spread * noise) if base else spread * noise
        out[name] = __import__('jax').numpy.asarray(drawn.astype(out[name].dtype))
    for name, factor in factors.items():
        out[name] = (out[name] * factor).astype(out[name].dtype)
    return out
```

```python
import math
from contextlib import ExitStack

import numpy as np

import concourse.bass as bass
from concourse import mybir

F32 = mybir.dt.float32
F32R = mybir.dt.float32r
ALU = mybir.AluOpType
ACT = mybir.ActivationFunctionType
AX = mybir.AxisListType.X

P = 128
D = 2048
TOK = 256
WIDE = 2 * TOK
KT = D // P
LAYERS = 2
HEADS = 8
QK = 64
ALPHA = (2 * LAYERS) ** 0.25
LN_EPS = 1e-5
SUB_EPS = 1e-5
RMS_EPS = 1e-6
DIFF_SCALE = QK ** -0.5
HEAD_SCALE = P ** -0.5
WINDOWS = (2, 4, 8, 16)
LAM_INIT = [0.8 - 0.6 * math.exp(-0.3 * l) for l in range(LAYERS)]
MASKED = -1e30

UNIT = KT * P
HALF = UNIT // 2
SQUARE = 32
RAW_SLOTS = 4
SPLIT_SLOTS = 4
NMOD = 3 * D // P

U_MOD0 = 0
U_IN0 = 2 * KT
U_OUT0 = U_IN0 + 2 * 56
U_IN1 = U_OUT0 + 16 + 8
U_OUT1 = U_IN1 + 56
U_IN2 = U_OUT1 + 16
U_PROJ = U_IN2 + 80
U_OUT2 = U_PROJ + 16
U_MLP = U_OUT2 + 16
UNITS = U_MLP + 4 * 32

IN_SLOTS = [("q", 0), ("k", 0), ("v", 0), ("ag", 0), ("cu", 0), ("cc", 0), ("pu", 0),
            ("q", 1), ("k", 1), ("v", 1), ("ag", 1), ("cb", 1), ("cg", 1), ("pg", 1)]
IN2_SLOTS = ["qa", "ka", "va", "qb", "kb", "vb", "ga0", "ga1", "gb0", "gb1"]

VEC_COLS = {}
VEC_WIDTH = 0
for _name, _n in (("b_mod", LAYERS * NMOD), ("conv_w", LAYERS * 12), ("subln_g", LAYERS),
                  ("pool_scale", LAYERS * 4), ("ln_g", LAYERS * KT), ("ln_b", LAYERS * KT),
                  ("norm_mix_g", KT), ("norm_mlp_g", KT), ("norm_final_g", KT),
                  ("b_forget", HEADS), ("slope", HEADS), ("pool_edge", 4 * 16)):
    VEC_COLS[_name] = VEC_WIDTH
    VEC_WIDTH += _n


class InOrder:

    def __init__(self, engine, own):
        self.engine, self.own, self.base, self.count, self.last = engine, own, 0, 0, None

    def inc_own(self, instruction):
        instruction.then_inc(self.own, 1)
        self.count += 1
        self.last = (self.own, self.base + self.count)

    def inc(self, instruction, semaphore, value):
        instruction.then_inc(semaphore, 1)
        self.last = (semaphore, value)

    def wait_own(self):
        self.engine.wait_ge(*self.last)

    def enter_loop(self, i, steps):
        self.outer = (self.base, self.count, steps)
        self.base, self.count = self.base + self.count + i * steps, 0
        self.last = (self.own, self.base)

    def leave_loop(self, turns):
        base, count, steps = self.outer
        assert self.count == steps, f"the body takes {self.count} steps, not {steps}"
        self.base, self.count = base, count + turns * steps
        self.last = (self.own, self.base + self.count)


class Unit:

    def __init__(self, first, i, per, j):
        assert first % RAW_SLOTS == 0 and per % RAW_SLOTS == 0
        self.number = first + per * i + j
        self.slot = j % RAW_SLOTS
        self.wave = first // RAW_SLOTS + (per // RAW_SLOTS) * i + j // RAW_SLOTS
        self.exact = (first, i, per, j)

    def ahead(self, n):
        first, i, per, j = self.exact
        return Unit(first, i, per, j + n)


def two_blocks(nc, stream, tokens, cond, vectors, lam_in, pool_w, w_forget, rope, squares, tables, out):
    ctx = ExitStack()
    with ctx:
        at = [16512]

        def place(name, shape, dtype=F32, offset=None):
            here = at[0] if offset is None else offset
            if offset is None:
                at[0] += -(-4 * int(np.prod(shape)) // 32) * 32
                assert at[0] <= nc.sbuf_usable_end, (name, at[0] - nc.sbuf_usable_end)
            return nc.alloc_sbuf_tensor_at(name, [P, *shape], dtype, offset=here)

        def sem(name):
            return ctx.enter_context(nc.semaphore(name))

        raw = place("raw", [RAW_SLOTS, UNIT])
        w_hi = place("w_hi", [SPLIT_SLOTS, HALF], F32R)
        w_lo = place("w_lo", [SPLIT_SLOTS, HALF], F32R)
        x_at = at[0]
        x = place("x", [KT, 2, WIDE], F32R)
        xs = place("xs", [KT, 2, TOK], F32R, x_at)
        gates = place("gates", [2 * KT, TOK], F32, x_at + 4 * KT * WIDE)
        hidden = place("hidden", [KT, 2, TOK], F32R, x_at + 4 * KT * WIDE)
        res = place("res", [KT, WIDE])
        z = place("z", [2, WIDE])
        q_t = place("q_t", [WIDE])
        k_t = place("k_t", [WIDE])
        v_t = place("v_t", [WIDE])
        v_tok = place("v_tok", [4, P])
        work = place("work", [6, WIDE])
        a_t = place("a_t", [3, WIDE])
        se = place("se", [WIDE])
        shared_at = at[0]
        conv_in = place("conv_in", [2, TOK + 2])
        pad_a = place("pad_a", [2, TOK + 16])
        pad_b = place("pad_b", [2, TOK + 16])
        rope_sb = place("rope_sb", [2, TOK])
        shared_end = at[0]
        ident = place("ident", [P])
        mean_w = place("mean_w", [P])
        pool_sb = place("pool_sb", [P])
        vec = place("vec", [VEC_WIDTH])
        mod = place("mod", [LAYERS * NMOD, 2])
        cond_sb = place("cond_sb", [KT, 2])
        cond_e = place("cond_e", [KT, 2])
        cond_x = place("cond_x", [KT, SQUARE], F32R)
        mod_t = place("mod_t", [SQUARE])
        tiny = place("tiny", [64])
        table_sb = place("table_sb", [5, TOK], F32, shared_at)
        wf_raw = place("wf_raw", [KT, HEADS], F32, shared_at + 5120)
        wf_hi = place("wf_hi", [KT, HEADS], F32R, shared_at + 5632)
        wf_lo = place("wf_lo", [KT, HEADS], F32R, shared_at + 6144)
        log_f = place("log_f", [2, HEADS], F32, shared_at + 6656)
        log_t = place("log_t", [2, HEADS], F32, shared_at + 6720)
        cum_f = place("cum_f", [2, HEADS], F32, shared_at + 6784)
        log_b = place("log_b", [2, P], F32, shared_at + 6848)
        assert shared_at + 6848 + 1024 <= shared_end

        def vcol(name, i):
            return vec[:, bass.ds(VEC_COLS[name] + i, 1)]

        lam_col = [tiny[:, 4 * l + 3:4 * l + 4] for l in range(LAYERS)]
        eps_ln, eps_sub, eps_rms, one = (tiny[:, 8 + n:9 + n] for n in range(4))
        top = tiny[:, 16:24]
        top_s = tiny[:, 24:32]
        sums = tiny[:, 32:40]
        inv = tiny[:, 40:48]
        o_ss = tiny[:, 48:52]
        o_rs = tiny[:, 52:56]
        o_nw = tiny[:, 56:60]

        def probs(t, m):
            if t < 2:
                return work[:, 2 * t + m, :]
            return work[:, 4 + t - 2, TOK * m:TOK * (m + 1)]

        o_sb = work[:, 1, :]
        junk = work[:, 3, 0:P]
        sq = [work[:, 2, :], work[:, 3, :]]
        h_tmp = [work[:, 0, :], work[:, 1, :]]
        x_res = [work[:, 2, :], work[:, 3, :]]
        total = work[:, 4, :]
        rstd = work[:, 5, :]
        newton = a_t[:, 0, :]
        z_b = work[:, 0:2, :]

        def v_out(c):
            return work[:, 4 + c, :]

        banks = [ctx.enter_context(nc.psum_tensor(f"bank{n}", [P, WIDE], F32)) for n in range(8)]
        gemm_bank, att = banks[0:2], banks[2:8]

        raw_full = [sem(f"raw_full{n}") for n in range(RAW_SLOTS)]
        hi_done = sem("hi_done")
        lo_done = sem("lo_done")
        half_used = sem("half_used")
        z_full = sem("z_full")
        z_used = sem("z_used")
        z_sum = sem("z_sum")
        se_full = sem("se_full")
        h_full = sem("h_full")
        xhi_done = sem("xhi_done")
        x_full = sem("x_full")
        y_all = sem("y_all")
        s_done = sem("s_done")
        top_done = sem("top_done")
        exp_done = sem("exp_done")
        a_full = sem("a_full")
        t_done = sem("t_done")
        at_full = sem("at_full")
        vt_done = sem("vt_done")
        v_full = sem("v_full")
        o_done = sem("o_done")
        ss_full = sem("ss_full")
        o_full = sem("o_full")
        ot_done = sem("ot_done")
        pool_d = sem("pool_d")
        pool_mm = sem("pool_mm")
        pool_w_in = sem("pool_w_in")
        xres_in = [sem(f"xres_in{n}") for n in range(2)]
        sum_full = sem("sum_full")
        mu_done = sem("mu_done")
        cen_done = sem("cen_done")
        sq_full = sem("sq_full")
        sq_used = sem("sq_used")
        lnx_done = sem("lnx_done")
        scaled = sem("scaled")
        affine = sem("affine")
        rms_go = sem("rms_go")
        cond_in, const_in, tok_in, table_in = sem("cond_in"), sem("const_in"), sem("tok_in"), sem("table_in")
        cond_exp = sem("cond_exp")
        cond_hi = sem("cond_hi")
        cond_silu = sem("cond_silu")
        cond_full = sem("cond_full")
        lam_sum = sem("lam_sum")
        lam_exp = sem("lam_exp")
        memset_done = sem("memset_done")
        f_full = sem("f_full")
        f_hi = sem("f_hi")
        f_lo = sem("f_lo")
        f_mm = sem("f_mm")
        f_exp = sem("f_exp")
        f_in = sem("f_in")
        f_cum = sem("f_cum")
        lb_full = sem("lb_full")
        out_full = sem("out_full")
        out_in = sem("out_in")
        act_own, dve_own, pool_own = sem("act_own"), sem("dve_own"), sem("pool_own")

        def tiles(l, h):
            return 4 * h if l == 0 else 4 * HEADS + 2 * h

        def t_banks(l, h):
            return 3 * h if l == 0 else 3 * HEADS + 2 * h

        HEADS1 = LAYERS * HEADS
        TILES1 = tiles(1, HEADS)
        TBANKS1 = t_banks(1, HEADS)
        U_IN = [U_IN0, U_IN1]

        def in_slots(l):
            found = []
            for pair in range(1 if l == 0 else 2):
                for s, (kind, half) in enumerate(IN_SLOTS):
                    j = 2 * s if l == 0 else 14 * pair + s
                    found.append((j, kind, pair, half, l == 0 or kind in "kv"))
            return found

        block = ctx.enter_context(nc.Block())

        @block.sync
        def _(sp):
            def load(unit, waits=True):
                if waits:
                    sp.wait_ge(lo_done, 2 * (unit.number - RAW_SLOTS) + 2)
                sp.dma_start(raw[:, unit.slot, :], stream[unit.number]).then_inc(raw_full[unit.slot], 16)

            for j in range(RAW_SLOTS):
                load(Unit(0, 0, 4, j), waits=False)
            with sp.Fori(0, UNITS // RAW_SLOTS - 1) as i:
                for j in range(RAW_SLOTS):
                    load(Unit(RAW_SLOTS, i, RAW_SLOTS, j))
            with sp.Fori(0, KT // 2) as i:
                for b in range(2):
                    sp.wait_ge(out_full, 2 * i + b + 1)
                    sp.dma_start(out[:, 2 * i + b, :], res[:, 2 * i + b, TOK:WIDE]).then_inc(out_in, 16)
            sp.wait_ge(out_in, 16 * KT)

        @block.gpsimd
        def _(pool):
            own = InOrder(pool, pool_own)
            own.inc_own(pool.memset(pad_a[:], 0.0))

            def windows(l, g):
                n = 2 if l == 0 else 1
                done = 4 * l + g
                if done:
                    pool.wait_ge(pool_mm, done)
                pool.dma_start(pool_sb[:, :], pool_w[4 * l + g]).then_inc(pool_w_in, 16)
                j = 28 * g + 12 if l == 0 else 14 * g + 6
                pool.wait_ge(z_used, U_IN[l] + j + 1)
                row = res[:, 12 + g, (0 if l == 0 else TOK):WIDE].rearrange("p (n t) -> p n t", t=TOK)
                own.wait_own()
                for edge in (slice(0, 8), slice(TOK + 8, TOK + 16)):
                    own.inc_own(pool.memset(pad_a[:, 0:n, edge], 0.0))
                own.inc_own(pool.tensor_copy(pad_a[:, 0:n, 8:8 + TOK], row))
                src, dst = pad_a, pad_b
                lo, hi = 1, TOK + 16
                own.wait_own()
                own.inc_own(pool.tensor_tensor(dst[:, 0:n, lo:hi], src[:, 0:n, lo - 1:hi - 1], src[:, 0:n, lo:hi], ALU.add))
                for level in range(1, g + 1):
                    d = 1 << (level - 1)
                    src, dst = dst, src
                    lo, hi = lo + d, hi - d
                    own.wait_own()
                    own.inc_own(pool.tensor_tensor(dst[:, 0:n, lo:hi], src[:, 0:n, lo - d:hi - d],
                                                src[:, 0:n, lo + d:hi + d], ALU.add))
                assert lo <= 8 and hi >= 8 + TOK
                own.wait_own()
                own.inc_own(pool.tensor_scalar(dst[:, 0:n, 8:8 + TOK], dst[:, 0:n, 8:8 + TOK],
                                            1.0 / WINDOWS[g], 1.0, ALU.mult, ALU.mult))
                own.wait_own()
                for s in range(n):
                    for e, c in ((0, 8), (8, TOK)):
                        edge = vec[:, VEC_COLS["pool_edge"] + 16 * g + e:VEC_COLS["pool_edge"] + 16 * g + e + 8]
                        own.inc_own(pool.tensor_tensor(dst[:, s, c:c + 8], dst[:, s, c:c + 8], edge, ALU.mult))
                own.wait_own()
                own.inc(pool.tensor_tensor(row, dst[:, 0:n, 8:8 + TOK], row, ALU.subtract), pool_d, done + 1)

            pool.wait_ge(const_in, 16 * 5)
            for g in range(4):
                windows(0, g)
            for b in range(2):
                if b == 0:
                    pool.wait_ge(z_used, U_OUT0)
                    pool.wait_ge(o_full, HEADS)
                pool.dma_start(x_res[b], tokens[:, b, :]).then_inc(xres_in[b], 16)
            with pool.Fori(0, 3) as i:
                for b in range(2):
                    pool.wait_ge(z_used, U_OUT0 + 4 * i + 2 * b + 1)
                    pool.dma_start(x_res[b], tokens[:, 2 * i + b + 2, :]).then_inc(xres_in[b], 16)
            for b in range(2):
                pool.wait_ge(z_used, U_OUT0 + 12 + 2 * b + 1)
                pool.dma_start(x_res[b], tokens[:, 8 + b, :]).then_inc(xres_in[b], 16)
            with pool.Fori(0, 3) as i:
                for b in range(2):
                    pool.wait_ge(z_used, U_OUT0 + 16 + 2 * i + b + 1)
                    pool.dma_start(x_res[b], tokens[:, 2 * i + b + 10, :]).then_inc(xres_in[b], 16)
            for g in range(4):
                windows(1, g)

        @block.scalar
        def _(act):
            own = InOrder(act, act_own)
            act.dma_start(cond_sb[:], cond).then_inc(cond_in, 16)
            act.dma_start(vec[:], vectors).then_inc(const_in, 16)
            act.dma_start(ident[:], squares[:, 0]).then_inc(const_in, 16)
            act.dma_start(work[:, 0, :], lam_in).then_inc(const_in, 16)
            act.dma_start(rope_sb[:], rope).then_inc(const_in, 16)
            act.dma_start(mean_w[:], squares[:, 1]).then_inc(const_in, 16)
            act.dma_start(res[:], tokens).then_inc(tok_in, 16)

            def round_half(unit, g):
                if g == 0:
                    act.wait_ge(raw_full[unit.slot], 16 * (unit.wave + 1))
                if unit.exact[3] >= 2 or unit.exact[0] > 0 or not isinstance(unit.exact[1], int):
                    act.wait_ge(half_used, 2 * unit.number + g + 1 - SPLIT_SLOTS)
                own.inc(act.activation(w_hi[:, 2 * (unit.slot % 2) + g, :],
                                          raw[:, unit.slot, g * HALF:(g + 1) * HALF], ACT.Copy),
                           hi_done, 2 * unit.number + g + 1)

            def take(unit, width=WIDE):
                act.wait_ge(half_used, 2 * unit.number + 2)
                if unit.exact[3] >= 2 or unit.exact[0] > 0 or not isinstance(unit.exact[1], int):
                    act.wait_ge(z_used, unit.number - 1)
                b = unit.slot % 2
                rows = SQUARE if width == P else P
                own.inc(act.activation(z[0:rows, b, 0:width], gemm_bank[b][0:rows, 0:width], ACT.Copy),
                           z_full, unit.number + 1)

            def slot(unit, width=WIDE, gate=None, wide=True, after=None, last=False):
                if not last:
                    round_half(unit.ahead(2), 0)
                take(unit, width)
                if gate is not None:
                    if wide:
                        own.wait_own()
                    else:
                        act.wait_ge(z_sum, gate - 16 + 1)
                    t = WIDE if wide else TOK
                    own.inc(act.activation(se[:, 0:t], z[:, unit.slot % 2, 0:t], ACT.Exp, scale=-1.0),
                               se_full, gate + 1)
                if not last:
                    round_half(unit.ahead(2), 1)
                if after:
                    after()

            act.wait_ge(cond_in, 16)
            act.activation(cond_e[:], cond_sb[:], ACT.Exp, scale=-1.0).then_inc(cond_exp, 1)
            act.wait_ge(cond_silu, 1)
            act.activation(cond_x[:, :, 0:2], cond_sb[:], ACT.Copy).then_inc(cond_hi, 1)
            act.wait_ge(lam_sum, 1)
            for l in range(LAYERS):
                last = act.activation(tiny[:, 4 * l:4 * l + 2], tiny[:, 4 * l:4 * l + 2], ACT.Exp)
            last.then_inc(lam_exp, 1)

            for j in range(2):
                round_half(Unit(0, 0, 4, j), 0)
                round_half(Unit(0, 0, 4, j), 1)
            for j in range(4):
                slot(Unit(0, 0, 4, j), width=P)
            with act.Fori(0, U_IN0 // 4 - 1) as i:
                own.enter_loop(i, 0)
                for j in range(4):
                    slot(Unit(4, i, 4, j), width=P)
                own.leave_loop(U_IN0 // 4 - 1)

            def split_x(phase, source, target, t, ready):
                with act.Fori(0, KT // 2) as i:
                    own.enter_loop(i, 0)
                    for b in range(2):
                        ready(2 * i + b, i, b)
                        act.activation(target[:, 2 * i + b, 0, 0:t], source(i, b), ACT.Copy)\
                           .then_inc(xhi_done, 1)
                    own.leave_loop(KT // 2)

            def from_h(n):
                return lambda k, i, b: act.wait_ge(h_full, 16 * n + k + 1)

            def softmax(count, t_list):
                for n, t in enumerate(t_list):
                    act.wait_ge(top_done, count + n + 1)
                    for m in range(2):
                        last = act.activation(probs(t, m), scores(t, m), ACT.Exp, bias=top_s[:, 2 * t + m:2 * t + m + 1],
                                              scale=DIFF_SCALE, accum_out=sums[:, 2 * t + m:2 * t + m + 1])
                    own.inc(last, exp_done, count + n + 1)

            def scores(t, m):
                return att[2 * t + m][:, :] if t < 2 else att[4 + m][:, TOK * (t - 2):TOK * (t - 1)]

            def layer_in(l):
                n_tiles = 4 if l == 0 else 2
                steps = 10 if l == 0 else 12

                with act.Fori(0, 4 if l == 0 else 2) as i:
                    own.enter_loop(i, steps)
                    for j, kind, pair, half, wide in in_slots(l):
                        p = i if l == 0 else 2 * i + pair
                        h = 2 * p + half
                        unit = Unit(U_IN[l], i, 28, j)
                        gate = {"ag": half, "cg": 2, "pg": 3}.get(kind)
                        if gate is not None:
                            gate = 16 * l + 4 * p + gate

                        def after():
                            if kind == "v":
                                softmax(tiles(l, h), range(n_tiles))
                            elif kind == "ag":
                                act.wait_ge(vt_done, 8 * l + h + 1)
                                own.inc(act.activation(v_tok[:].rearrange("p a b -> p (a b)"), att[5][:, :], ACT.Copy),
                                           v_full, 8 * l + h + 1)
                            elif kind in ("cu", "cb"):
                                n = 3 if l == 0 else 2
                                for c in range(n):
                                    act.wait_ge(t_done, t_banks(l, h) + c + 1)
                                    own.inc(act.activation(a_t[:, c, :], att[c][:, :], ACT.Copy),
                                               at_full, t_banks(l, h) + c + 1)
                            elif kind in ("cc", "cg"):
                                act.wait_ge(o_done, 8 * l + h + 1)
                                for t in range(n_tiles):
                                    if t:
                                        own.wait_own()
                                    own.inc_own(act.activation(junk, att[3][:, P * t:P * (t + 1)], ACT.Square,
                                                            accum_out=o_ss[:, t:t + 1]))
                                own.wait_own()
                                own.inc_own(act.activation(o_rs[:, 0:n_tiles], o_ss[:, 0:n_tiles], ACT.Ln,
                                                        scale=1.0 / P, bias=eps_sub))
                                own.wait_own()
                                own.inc(act.activation(o_rs[:, 0:n_tiles], o_rs[:, 0:n_tiles], ACT.Exp, scale=-0.5),
                                           ss_full, 8 * l + h + 1)
                        slot(unit, gate=gate, wide=wide, after=after)
                        if l == 0:
                            slot(unit.ahead(1), width=P)
                    own.leave_loop(4 if l == 0 else 2)

            def rough_rsqrt(t, eps, n):
                act.wait_ge(sq_used, 16 * n + 16)
                own.inc_own(act.activation(rstd[:, 0:t], att[1][:, 0:t], ACT.Ln, bias=eps))
                own.wait_own()
                own.inc(act.activation(rstd[:, 0:t], rstd[:, 0:t], ACT.Exp, scale=-0.5), lnx_done, n + 1)

            def squares_of(n, t, centred):
                for k in range(KT):
                    if centred:
                        act.wait_ge(cen_done, 16 * centred - 16 + k + 1)
                    if k >= 2:
                        act.wait_ge(sq_used, 16 * n + k - 1)
                    act.activation(sq[k % 2][:, 0:t], res[:, k, 0:t], ACT.Square).then_inc(sq_full, 1)

            def layer_out(l, first, halves):
                for begin, turns, mods in halves:
                    with act.Fori(0, turns) as i:
                        own.enter_loop(i, 0)
                        for j in range(4):
                            unit = Unit(begin, i, 4, j)
                            slot(unit, width=P if mods and j % 2 else WIDE)
                        own.leave_loop(turns)

            def norm(l, t, n):
                squares_of(n, t, l + 1)
                rough_rsqrt(t, eps_ln, n)
                with act.Fori(0, KT // 2) as i:
                    own.enter_loop(i, 0)
                    for b in range(2):
                        k = 2 * i + b
                        act.wait_ge(scaled, 16 * l + k + 1)
                        act.activation(res[:, k, 0:t], res[:, k, 0:t], ACT.Identity,
                                       scale=vcol("ln_g", 16 * l + k), bias=vcol("ln_b", 16 * l + k))\
                           .then_inc(affine, 1)
                    if l == 0:
                        for b in range(2):
                            k = 2 * i + b
                            act.wait_ge(h_full, 16 + k + 1)
                            act.activation(x[:, k, 0, :], h_tmp[b], ACT.Copy).then_inc(xhi_done, 1)
                    own.leave_loop(KT // 2)

            def split_h(n, target, t, unit_before):
                act.wait_ge(half_used, 2 * unit_before)
                with act.Fori(0, KT // 2) as i:
                    own.enter_loop(i, 0)
                    for b in range(2):
                        k = 2 * i + b
                        act.wait_ge(h_full, 16 * n + k + 1)
                        act.activation(target[:, k, 0, 0:t], h_tmp[b][:, 0:t], ACT.Copy).then_inc(xhi_done, 1)
                    own.leave_loop(KT // 2)

            def split_y(n, target, cols, unit_before):
                act.wait_ge(half_used, 2 * unit_before)
                act.wait_ge(y_all, n)
                t = cols.stop - cols.start
                with act.Fori(0, KT) as k:
                    own.enter_loop(k, 0)
                    act.activation(target[:, k, 0, 0:t], res[:, k, cols], ACT.Copy).then_inc(xhi_done, 1)
                    own.leave_loop(KT)

            split_h(0, x, WIDE, U_IN0)
            layer_in(0)
            split_y(1, x, slice(0, WIDE), U_OUT0)
            layer_out(0, U_OUT0, [(U_OUT0, 4, True), (U_OUT0 + 16, 2, False)])
            norm(0, WIDE, 0)
            layer_in(1)
            split_y(2, x, slice(TOK, WIDE), U_OUT1)
            layer_out(1, U_OUT1, [(U_OUT1, 4, False)])
            norm(1, TOK, 1)

            act.dma_start(table_sb[:], tables).then_inc(table_in, 16)
            act.dma_start(wf_raw[:], w_forget).then_inc(table_in, 16)
            act.wait_ge(table_in, 32)
            act.activation(wf_hi[:], wf_raw[:], ACT.Copy).then_inc(f_hi, 1)
            act.wait_ge(rms_go, 1)
            squares_of(2, TOK, None)
            rough_rsqrt(TOK, eps_rms, 2)
            split_h(2, xs, TOK, U_IN2)

            act.wait_ge(f_in, 1)
            own.inc_own(act.activation(log_t[:], log_t[:], ACT.Exp, scale=-1.0))
            own.wait_own()
            own.inc(act.activation(log_t[:], log_t[:], ACT.Ln, bias=one), f_exp, 1)

            def softmax2(p, kind):
                count = TILES1 + 2 * p + kind
                act.wait_ge(top_done, count + 1)
                for t in range(2):
                    keys = P * (t + 1)
                    last = act.activation(work[:, 2 * kind + t, 0:keys], work[:, 2 * kind + t, 0:keys], ACT.Exp,
                                          bias=top_s[:, 2 * kind + t:2 * kind + t + 1], scale=HEAD_SCALE,
                                          accum_out=sums[:, 2 * kind + t:2 * kind + t + 1])
                own.inc(last, exp_done, count + 1)

            with act.Fori(0, 4) as i:
                own.enter_loop(i, 0)
                for half in range(2):
                    p = 2 * i + half
                    for s, kind in enumerate(IN2_SLOTS):
                        unit = Unit(U_IN2, i, 20, 10 * half + s)

                        def after():
                            if kind in ("va", "vb"):
                                c = kind == "vb"
                                act.wait_ge(vt_done, HEADS1 + 2 * p + c + 1)
                                own.inc(act.activation(v_tok[:, 2 * c:2 * c + 2, :].rearrange("p a b -> p (a b)"),
                                                          att[5][:, 0:2 * P], ACT.Copy), v_full, HEADS1 + 2 * p + c + 1)
                                softmax2(p, c)
                            elif kind in ("qb", "ga0"):
                                c = kind == "ga0"
                                act.wait_ge(t_done, TBANKS1 + 2 * p + c + 1)
                                own.inc(act.activation(a_t[:, c, 0:3 * P], att[2][:, 0:3 * P], ACT.Copy),
                                           at_full, TBANKS1 + 2 * p + c + 1)
                        gate = 32 + 4 * p + s - 6 if s >= 6 else None
                        slot(unit, gate=gate, wide=False, after=after)
                own.leave_loop(4)

            split_y(3, xs, slice(TOK, WIDE), U_PROJ)
            with act.Fori(0, 4) as i:
                own.enter_loop(i, 0)
                for j in range(4):
                    unit = Unit(U_PROJ, i, 4, j)
                    round_half(unit.ahead(2), 0)
                    act.wait_ge(half_used, 2 * unit.number + 2)
                    act.wait_ge(z_used, unit.number - 1)
                    act.activation(z_b[:, j % 2, :], att[j % 2][:, :], ACT.Copy)
                    own.inc(act.activation(z[:, j % 2, :], gemm_bank[j % 2][:, :], ACT.Copy),
                               z_full, unit.number + 1)
                    round_half(unit.ahead(2), 1)
                own.leave_loop(4)
            split_y(4, xs, slice(TOK, WIDE), U_OUT2)
            layer_out(2, U_OUT2, [(U_OUT2, 4, False)])
            act.wait_ge(rms_go, 2)
            squares_of(3, TOK, None)
            rough_rsqrt(TOK, eps_rms, 3)
            split_h(3, xs, TOK, U_MLP)

            def up(first, c):
                with act.Fori(0, 4) as i:
                    own.enter_loop(i, 0)
                    for j in range(4):
                        unit = Unit(first, i, 4, j)
                        k = 4 * i + j

                        def after():
                            act.wait_ge(h_full, 64 + 16 * c + k + 1)
                            act.activation(hidden[:, k, 0, :], h_tmp[0][:, 0:TOK], ACT.Copy).then_inc(xhi_done, 1)
                        slot(unit, after=after)
                    own.leave_loop(4)

            for c in range(4):
                up(U_MLP + 32 * c, c)
                if c < 3:
                    layer_out(3, 0, [(U_MLP + 32 * c + 16, 4, False)])
                else:
                    layer_out(3, 0, [(U_MLP + 32 * c + 16, 3, False)])
                    for j in range(4):
                        slot(Unit(UNITS - 4, 0, 4, j), last=j >= 2)
            act.wait_ge(rms_go, 3)
            squares_of(4, TOK, None)
            rough_rsqrt(TOK, eps_rms, 4)

        @block.vector
        def _(dve):
            own = InOrder(dve, dve_own)

            def tt(o, a, b, op):
                own.inc_own(dve.tensor_tensor(o, a, b, op))

            def ts(o, a, s1, op0, s2=None, op1=None):
                if op1 is None:
                    own.inc_own(dve.tensor_scalar(o, a, s1, None, op0))
                else:
                    own.inc_own(dve.tensor_scalar(o, a, s1, s2, op0, op1))

            def stt(o, a, s, b, op0, op1):
                own.inc_own(dve.scalar_tensor_tensor(out=o, in0=a, scalar=s, in1=b, op0=op0, op1=op1))

            def fence():
                own.inc_own(dve.memset(tiny[:, 60:61], 0.0))
                own.wait_own()

            def announce(semaphore, value):
                fence()
                own.inc(dve.memset(tiny[:, 62:63], 0.0), semaphore, value)
                own.wait_own()

            def rest_half(unit, g):
                dve.wait_ge(hi_done, 2 * unit.number + g + 1)
                n = 2 * (unit.slot % 2) + g
                own.inc(dve.tensor_tensor(w_lo[:, n, :], raw[:, unit.slot, g * HALF:(g + 1) * HALF],
                                             w_hi[:, n, :].bitcast(F32), ALU.subtract),
                           lo_done, 2 * unit.number + g + 1)

            def slot(unit, epilogue, before=None, after=None, last=False):
                if not last:
                    rest_half(unit.ahead(2), 0)
                if before:
                    before()
                dve.wait_ge(z_full, unit.number + 1)
                own.wait_own()
                own.inc(epilogue(z[:, unit.slot % 2, :]), z_used, unit.number + 1)
                if after:
                    after()
                if not last:
                    rest_half(unit.ahead(2), 1)

            def stt_i(o, a, s, b, op0, op1):
                return dve.scalar_tensor_tensor(out=o, in0=a, scalar=s, in1=b, op0=op0, op1=op1)

            dve.memset(conv_in[:], 0.0)
            dve.memset(cond_x[:].bitcast(F32), 0.0)
            dve.memset(eps_ln, LN_EPS)
            dve.memset(eps_sub, SUB_EPS)
            dve.memset(eps_rms, RMS_EPS)
            own.inc_own(dve.memset(one, 1.0))
            dve.wait_ge(cond_exp, 1)
            ts(cond_e[:], cond_e[:], 1.0, ALU.add)
            own.wait_own()
            own.inc_own(dve.reciprocal(cond_e[:], cond_e[:]))
            own.wait_own()
            own.inc(dve.tensor_tensor(cond_sb[:], cond_sb[:], cond_e[:], ALU.mult), cond_silu, 1)
            dve.wait_ge(cond_hi, 1)
            own.inc(dve.tensor_tensor(cond_x[:, :, 2:4], cond_sb[:], cond_x[:, :, 0:2].bitcast(F32), ALU.subtract),
                       cond_full, 1)
            dve.wait_ge(const_in, 16 * 5)
            lam_v = work[:, 0, :].rearrange("p (l v d) -> p l v d", l=LAYERS, v=4)
            for l in range(LAYERS):
                for m in range(2):
                    n = 2 * l + m
                    tt(work[:, 1, 64 * n:64 * n + 64], lam_v[:, l, 2 * m, :], lam_v[:, l, 2 * m + 1, :], ALU.mult)
            own.wait_own()
            for l in range(LAYERS):
                last = dve.reduce_sum(tiny[:, 4 * l:4 * l + 2],
                                      work[:, 1, 128 * l:128 * l + 128].rearrange("p (m d) -> p m d", m=2), axis=AX)
            own.inc(last, lam_sum, 1)
            dve.wait_ge(lam_exp, 1)
            for l in range(LAYERS):
                tt(tiny[:, 4 * l + 2:4 * l + 3], tiny[:, 4 * l + 1:4 * l + 2], tiny[:, 4 * l:4 * l + 1], ALU.subtract)
                own.wait_own()
                ts(tiny[:, 4 * l + 3:4 * l + 4], tiny[:, 4 * l + 2:4 * l + 3], -LAM_INIT[l], ALU.add)
                ts(vcol("subln_g", l), vcol("subln_g", l), 1.0 - LAM_INIT[l], ALU.mult)

            for j in range(2):
                rest_half(Unit(0, 0, 4, j), 0)
                rest_half(Unit(0, 0, 4, j), 1)

            def modulation(m):
                def epilogue(zz):
                    for c in range(P // SQUARE):
                        rows = slice(SQUARE * c, SQUARE * (c + 1))
                        last = dve.transpose(mod_t[rows, :], zz[0:SQUARE, rows])
                    own.inc_own(last)
                    own.wait_own()
                    return stt_i(mod[:, m, :], mod_t[:, 0:2], vcol("b_mod", m), mod_t[:, 2:4], ALU.add, ALU.add)
                return epilogue

            for j in range(4):
                slot(Unit(0, 0, 4, j), modulation(j))
            with dve.Fori(0, U_IN0 // 4 - 1) as i:
                own.enter_loop(i, STEPS["mod"])
                for j in range(4):
                    slot(Unit(4, i, 4, j), modulation(4 * i + 4 + j))
                own.leave_loop(U_IN0 // 4 - 1)

            def scale_up(l):
                fence()
                s = mod[:, NMOD * l + KT:NMOD * l + 2 * KT, :]
                ts(s, s, 1.0, ALU.add)
                own.wait_own()

            def modulate(l, k, b):
                for s in range(2):
                    cols = slice(TOK * s, TOK * (s + 1))
                    last = dve.tensor_scalar(h_tmp[b][:, cols], res[:, k, cols],
                                             mod[:, NMOD * l + KT + k, s:s + 1], mod[:, NMOD * l + k, s:s + 1],
                                             ALU.mult, ALU.add)
                own.inc(last, h_full, 16 * l + k + 1)

            def rest_x(n, k, source, target, t):
                dve.wait_ge(xhi_done, 16 * n + k + 1)
                own.inc(dve.tensor_tensor(target[:, k, 1, 0:t], source, target[:, k, 0, 0:t].bitcast(F32),
                                             ALU.subtract), x_full, 16 * n + k + 1)

            def split_y(n, target, cols):
                with dve.Fori(0, KT) as k:
                    own.enter_loop(k, 0)
                    rest_x(n, k, res[:, k, cols], target, cols.stop - cols.start)
                    own.leave_loop(KT)

            scale_up(0)
            dve.wait_ge(tok_in, 16)
            with dve.Fori(0, KT // 2) as i:
                own.enter_loop(i, 0)
                for b in range(2):
                    modulate(0, 2 * i + b, b)
                for b in range(2):
                    rest_x(0, 2 * i + b, h_tmp[b], x, WIDE)
                dve.wait_ge(x_full, 2 * i + 2)
                own.leave_loop(KT // 2)

            def scores(t, m):
                return att[2 * t + m][:, :] if t < 2 else att[4 + m][:, TOK * (t - 2):TOK * (t - 1)]

            def layer_in(l, steps):
                n_tiles = 4 if l == 0 else 2
                ycols = slice(0, WIDE) if l == 0 else slice(TOK, WIDE)
                t_y = ycols.stop - ycols.start
                nseq = t_y // TOK

                def seq(ap):
                    return ap.rearrange("p (n t) -> p n t", t=TOK)

                with dve.Fori(0, 4 if l == 0 else 2) as i:
                    own.enter_loop(i, steps)
                    for j, kind, pair, half, wide in in_slots(l):
                        p = i if l == 0 else 2 * i + pair
                        h = 2 * p + half
                        hh = 8 * l + h
                        unit = Unit(U_IN[l], i, 28, j)
                        gate = {"ag": half, "cg": 2, "pg": 3}.get(kind)
                        if gate is not None:
                            gate = 16 * l + 4 * p + gate

                        def silu(zz):
                            dve.wait_ge(se_full, gate + 1)
                            ts(se[:, 0:t_y], se[:, 0:t_y], 1.0, ALU.add)
                            own.wait_own()
                            own.inc_own(dve.reciprocal(se[:, 0:t_y], se[:, 0:t_y]))
                            own.wait_own()

                        def epilogue(zz):
                            if not wide:
                                ins = dve.tensor_tensor(zz[:, 0:TOK], zz[:, 0:TOK], zz[:, TOK:WIDE], ALU.add)
                                if gate is None:
                                    own.inc_own(ins)
                                else:
                                    own.inc(ins, z_sum, gate - 16 + 1)
                                own.wait_own()
                            zt = zz[:, 0:t_y]
                            if kind in ("q", "k"):
                                dst = q_t if kind == "q" else k_t
                                tt(dst[:, 0:TOK], zz[:, 0:TOK], rope_sb[:, 0, :], ALU.mult)
                                own.inc_own(dve.stream_shuffle(se[:, 0:TOK], zz[:, 0:TOK],
                                                            [(n + 16) % 32 for n in range(32)]))
                                if wide:
                                    own.inc_own(dve.tensor_copy(dst[:, TOK:WIDE], zz[:, TOK:WIDE]))
                                own.wait_own()
                                tt(se[:, 0:TOK], se[:, 0:TOK], rope_sb[:, 1, :], ALU.mult)
                                own.wait_own()
                                return dve.tensor_tensor(dst[:, 0:TOK], dst[:, 0:TOK], se[:, 0:TOK], ALU.add)
                            if kind == "v":
                                return dve.tensor_copy(v_t[:, :], zz)
                            if kind == "ag":
                                silu(zt)
                                return stt_i(res[:, 4 + h, ycols], se[:, 0:t_y], vcol("subln_g", l), zt, ALU.mult, ALU.mult)
                            if kind == "cu":
                                return dve.tensor_copy(res[:, p, ycols], zt)
                            y = res[:, p, ycols]
                            if kind == "cc":
                                tt(conv_in[:, 0:nseq, 1:TOK + 1], seq(zt), seq(y), ALU.mult)
                                own.wait_own()
                                w = [vcol("conv_w", 12 * l + 4 * c + p) for c in range(3)]
                                ts(seq(y), conv_in[:, 0:nseq, 0:TOK], w[0], ALU.mult)
                                own.wait_own()
                                stt(seq(y), conv_in[:, 0:nseq, 1:TOK + 1], w[1], seq(y), ALU.mult, ALU.add)
                                own.wait_own()
                                return stt_i(seq(y), conv_in[:, 0:nseq, 2:TOK + 2], w[2], seq(y), ALU.mult, ALU.add)
                            if kind == "cb":
                                return dve.tensor_tensor(y, y, zt, ALU.mult)
                            if kind == "cg":
                                silu(zt)
                                tt(se[:, 0:t_y], se[:, 0:t_y], zt, ALU.mult)
                                own.wait_own()
                                return dve.tensor_tensor(y, y, se[:, 0:t_y], ALU.mult)
                            y = res[:, 12 + p, ycols]
                            if kind == "pu":
                                return dve.tensor_copy(y, zt)
                            silu(zt)
                            tt(se[:, 0:t_y], se[:, 0:t_y], zt, ALU.mult)
                            dve.wait_ge(pool_mm, 4 * l + p + 1)
                            own.wait_own()
                            return stt_i(y, att[5][:, 0:t_y], vcol("pool_scale", 4 * l + p), se[:, 0:t_y],
                                         ALU.mult, ALU.mult)

                        def before():
                            if kind == "ag":
                                for t in range(n_tiles):
                                    dve.wait_ge(exp_done, tiles(l, h) + t + 1)
                                    own.inc_own(dve.reciprocal(inv[:, 2 * t:2 * t + 2], sums[:, 2 * t:2 * t + 2]))
                                    own.wait_own()
                                    tt(inv[:, 2 * t + 1:2 * t + 2], inv[:, 2 * t + 1:2 * t + 2], lam_col[l], ALU.mult)
                                    ts(probs(t, 0), probs(t, 0), inv[:, 2 * t:2 * t + 1], ALU.mult)
                                    own.wait_own()
                                    own.inc(stt_i(probs(t, 0), probs(t, 1), inv[:, 2 * t + 1:2 * t + 2], probs(t, 0),
                                                     ALU.mult, ALU.add), a_full, tiles(l, h) + t + 1)

                        def after():
                            if kind == "v":
                                for group in ((0,), (1,), (2, 3))[:n_tiles - 1 if l == 0 else 2]:
                                    dve.wait_ge(s_done, tiles(l, h) + group[-1] + 1)
                                    for t in group:
                                        for m in range(2):
                                            own.inc_own(dve.reduce_max(top[:, 2 * t + m:2 * t + m + 1], scores(t, m), axis=AX))
                                    own.wait_own()
                                    for t in group:
                                        own.inc(dve.tensor_scalar(top_s[:, 2 * t:2 * t + 2], top[:, 2 * t:2 * t + 2],
                                                                     -DIFF_SCALE, None, ALU.mult),
                                                   top_done, tiles(l, h) + t + 1)
                            elif kind in ("cc", "cg"):
                                dve.wait_ge(ss_full, hh + 1)
                                n = n_tiles
                                tt(o_nw[:, 0:n], o_rs[:, 0:n], o_rs[:, 0:n], ALU.mult)
                                ts(o_ss[:, 0:n], o_ss[:, 0:n], 1.0 / P, ALU.mult, SUB_EPS, ALU.add)
                                own.wait_own()
                                tt(o_nw[:, 0:n], o_nw[:, 0:n], o_ss[:, 0:n], ALU.mult)
                                own.wait_own()
                                ts(o_nw[:, 0:n], o_nw[:, 0:n], -0.5, ALU.mult, 1.5, ALU.add)
                                own.wait_own()
                                tt(o_rs[:, 0:n], o_rs[:, 0:n], o_nw[:, 0:n], ALU.mult)
                                own.wait_own()
                                for t in range(n):
                                    last = dve.tensor_scalar(o_sb[:, P * t:P * (t + 1)], att[3][:, P * t:P * (t + 1)],
                                                             o_rs[:, t:t + 1], None, ALU.mult)
                                own.inc(last, o_full, hh + 1)
                            elif kind in ("pu", "pg"):
                                dve.wait_ge(ot_done, hh + 1)
                                y = res[:, 4 + h, ycols]
                                tt(y, att[4][:, 0:t_y], y, ALU.mult)
                        slot(unit, epilogue, before, after)
                        if l == 0:
                            slot(unit.ahead(1), modulation(2 * KT + 14 * i + j // 2))
                    own.leave_loop(4 if l == 0 else 2)
                announce(y_all, l + 1)

            def layer_out(l, begin, turns, k0, mods, steps):
                with dve.Fori(0, turns) as i:
                    own.enter_loop(i, steps)
                    for j in range(4):
                        unit = Unit(begin, i, 4, j)
                        if mods and j % 2:
                            slot(unit, modulation(LAYERS * NMOD - 8 + 2 * i + j // 2))
                            continue
                        k = k0 + (2 * i + j // 2 if mods else 4 * i + j)

                        def epilogue(zz):
                            if l == 0:
                                b = (j // 2 if mods else j) % 2
                                wave = (k0 // 2 + i) if mods else (k0 // 2 + 2 * i + j // 2)
                                dve.wait_ge(xres_in[b], 16 * (wave + 1))
                                for s in range(2):
                                    cols = slice(TOK * s, TOK * (s + 1))
                                    ts(zz[:, cols], zz[:, cols], mod[:, 2 * KT + k, s:s + 1], ALU.mult)
                                own.wait_own()
                                stt(res[:, k, :], x_res[b], ALPHA, zz, ALU.mult, ALU.add)
                                own.wait_own()
                                return dve.tensor_tensor(total, total, res[:, k, :], ALU.add)
                            tt(zz[:, 0:TOK], zz[:, 0:TOK], zz[:, TOK:WIDE], ALU.add)
                            own.wait_own()
                            r = res[:, k, 0:TOK]
                            if l == 1:
                                ts(zz[:, 0:TOK], zz[:, 0:TOK], mod[:, NMOD + 2 * KT + k, 0:1], ALU.mult)
                                own.wait_own()
                                stt(r, r, ALPHA, zz[:, 0:TOK], ALU.mult, ALU.add)
                                own.wait_own()
                                return dve.tensor_tensor(total[:, 0:TOK], total[:, 0:TOK], r, ALU.add)
                            return dve.tensor_tensor(r, r, zz[:, 0:TOK], ALU.add)
                        slot(unit, epilogue)
                    own.leave_loop(turns)

            def finish_rsqrt(t, eps, n):
                dve.wait_ge(lnx_done, n + 1)
                tt(newton[:, 0:t], rstd[:, 0:t], rstd[:, 0:t], ALU.mult)
                own.wait_own()
                stt(newton[:, 0:t], att[1][:, 0:t], eps, newton[:, 0:t], ALU.add, ALU.mult)
                own.wait_own()
                ts(newton[:, 0:t], newton[:, 0:t], -0.5, ALU.mult, 1.5, ALU.add)
                own.wait_own()
                tt(rstd[:, 0:t], rstd[:, 0:t], newton[:, 0:t], ALU.mult)
                own.wait_own()

            def norm(l, t):
                announce(sum_full, l + 1)
                dve.wait_ge(mu_done, l + 1)
                for k in range(KT):
                    own.inc(dve.tensor_tensor(res[:, k, 0:t], res[:, k, 0:t], att[0][:, 0:t], ALU.subtract),
                               cen_done, 16 * l + k + 1)
                finish_rsqrt(t, LN_EPS, l)
                if l == 0:
                    scale_up(1)
                with dve.Fori(0, KT // 2) as i:
                    own.enter_loop(i, 0)
                    for b in range(2):
                        k = 2 * i + b
                        own.inc(dve.tensor_tensor(res[:, k, 0:t], res[:, k, 0:t], rstd[:, 0:t], ALU.mult),
                                   scaled, 16 * l + k + 1)
                    if l == 0:
                        dve.wait_ge(x_full, 32 + 2 * i)
                        for b in range(2):
                            dve.wait_ge(affine, 2 * i + b + 1)
                            modulate(1, 2 * i + b, b)
                        for b in range(2):
                            rest_x(2, 2 * i + b, h_tmp[b], x, WIDE)
                    own.leave_loop(KT // 2)

            def normed(n, gain, target, phase, h_base):
                with dve.Fori(0, KT // 2) as i:
                    own.enter_loop(i, 0)
                    dve.wait_ge(x_full, 16 * phase + 2 * i)
                    for b in range(2):
                        k = 2 * i + b
                        own.inc(stt_i(h_tmp[b][:, 0:TOK], res[:, k, 0:TOK], vcol(gain, k), rstd[:, 0:TOK],
                                         ALU.mult, ALU.mult), h_full, h_base + k + 1)
                    for b in range(2):
                        rest_x(phase, 2 * i + b, h_tmp[b][:, 0:TOK], target, TOK)
                    own.leave_loop(KT // 2)

            layer_in(0, STEPS["in0"])
            split_y(1, x, slice(0, WIDE))
            dve.wait_ge(o_full, HEADS)
            own.inc_own(dve.memset(total, 0.0))
            layer_out(0, U_OUT0, 4, 0, True, STEPS["out0a"])
            layer_out(0, U_OUT0 + 16, 2, 8, False, STEPS["out0b"])
            norm(0, WIDE)
            layer_in(1, STEPS["in1"])
            split_y(3, x, slice(TOK, WIDE))
            own.inc_own(dve.memset(total, 0.0))
            layer_out(1, U_OUT1, 4, 0, False, STEPS["out1"])
            norm(1, TOK)

            dve.wait_ge(affine, 32)
            announce(rms_go, 1)
            dve.wait_ge(f_hi, 1)
            own.inc(dve.tensor_tensor(wf_lo[:], wf_raw[:], wf_hi[:].bitcast(F32), ALU.subtract), f_lo, 1)
            finish_rsqrt(TOK, RMS_EPS, 2)
            normed(2, "norm_mix_g", xs, 4, 32)

            dve.wait_ge(f_mm, 1)
            bias = vec[:, VEC_COLS["b_forget"]:VEC_COLS["b_forget"] + HEADS]
            for t in range(2):
                tt(log_f[:, t, :], att[3][:, HEADS * t:HEADS * (t + 1)], bias, ALU.add)
            own.wait_own()
            ts(log_t[:], log_f[:], -1.0, ALU.mult)
            own.wait_own()
            own.inc(dve.tensor_tensor(log_t[:], log_t[:], log_f[:], ALU.max), f_in, 1)
            ts(log_f[:], log_f[:], 0.0, ALU.min)
            dve.wait_ge(f_exp, 1)
            own.wait_own()
            own.inc(dve.tensor_tensor(log_f[:], log_f[:], log_t[:], ALU.subtract), f_full, 1)
            dve.wait_ge(f_cum, 1)
            ts(cum_f[:].rearrange("p t h -> p (t h)"), att[4][:, 0:2 * HEADS], 1.0 / HEAD_SCALE, ALU.mult)
            ts(log_f[:], log_f[:], -1.0 / HEAD_SCALE, ALU.mult)
            own.wait_own()
            ts(vec[:, VEC_COLS["slope"]:VEC_COLS["slope"] + HEADS], vec[:, VEC_COLS["slope"]:VEC_COLS["slope"] + HEADS],
               1.0 / HEAD_SCALE, ALU.mult)

            with dve.Fori(0, 4) as i:
                own.enter_loop(i, STEPS["in2"])
                for half in range(2):
                    p = 2 * i + half
                    for s, kind in enumerate(IN2_SLOTS):
                        unit = Unit(U_IN2, i, 20, 10 * half + s)
                        gate = 32 + 4 * p + s - 6 if s >= 6 else None
                        c = int(kind[1] == "b")

                        def epilogue(zz):
                            add = (zz[:, 0:TOK], zz[:, TOK:WIDE], ALU.add)
                            cols = slice(TOK * c, TOK * (c + 1))
                            if kind[0] in "qk":
                                return dve.tensor_tensor((q_t if kind[0] == "q" else k_t)[:, cols], *add)
                            if kind[0] == "v":
                                return dve.tensor_tensor(v_t[:, cols], *add)
                            own.inc(dve.tensor_tensor(zz[:, 0:TOK], *add), z_sum, gate - 16 + 1)
                            dve.wait_ge(se_full, gate + 1)
                            ts(se[:, 0:TOK], se[:, 0:TOK], 1.0, ALU.add)
                            own.wait_own()
                            return dve.reciprocal(gates[:, KT * c + 2 * p + s % 2, :], se[:, 0:TOK])

                        def before():
                            if kind == "ka":
                                for t in range(2):
                                    last = dve.tensor_scalar(log_b[:, t, :], table_sb[:, 4, P:2 * P],
                                                             log_f[:, t, bass.ds(p, 1)], None, ALU.mult)
                                own.inc(last, lb_full, p + 1)

                        def after():
                            if kind in ("va", "vb"):
                                count = TILES1 + 2 * p + c
                                dve.wait_ge(s_done, count + 1)
                                dve.wait_ge(ot_done, HEADS1 + 2 * p + c)
                                for t in range(2):
                                    keys = P * (t + 1)
                                    w = work[:, 2 * c + t, 0:keys]
                                    sc = att[c][:, TOK * t:TOK * t + keys]
                                    if c == 0:
                                        stt(w, table_sb[:, t, 0:keys], vcol("slope", p), sc, ALU.mult, ALU.add)
                                    else:
                                        stt(w, sc, cum_f[:, t, bass.ds(p, 1)], table_sb[:, 2 + t, 0:keys], ALU.add, ALU.add)
                                own.wait_own()
                                for t in range(2):
                                    own.inc_own(dve.reduce_max(top[:, 2 * c + t:2 * c + t + 1],
                                                            work[:, 2 * c + t, 0:P * (t + 1)], axis=AX))
                                own.wait_own()
                                own.inc(dve.tensor_scalar(top_s[:, 2 * c:2 * c + 2], top[:, 2 * c:2 * c + 2],
                                                             -HEAD_SCALE, None, ALU.mult), top_done, count + 1)
                            elif kind in ("kb", "ga1"):
                                c2 = int(kind == "ga1")
                                dve.wait_ge(exp_done, TILES1 + 2 * p + c2 + 1)
                                own.inc_own(dve.reciprocal(inv[:, 2 * c2:2 * c2 + 2], sums[:, 2 * c2:2 * c2 + 2]))
                                own.wait_own()
                                dve.wait_ge(o_done, HEADS1 + 2 * p + c2 + 1)
                                for t in range(2):
                                    last = dve.tensor_scalar(v_out(c2)[:, P * t:P * (t + 1)], att[3][:, P * t:P * (t + 1)],
                                                             inv[:, 2 * c2 + t:2 * c2 + t + 1], None, ALU.mult)
                                own.inc(last, o_full, HEADS1 + 2 * p + c2 + 1)
                            elif kind in ("gb0",):
                                dve.wait_ge(ot_done, HEADS1 + 2 * p + 2)
                                own.inc_own(dve.tensor_copy(res[:, HEADS + p, TOK:WIDE], att[4][:, 0:TOK]))
                        if kind == "ga0":
                            def before():
                                dve.wait_ge(ot_done, HEADS1 + 2 * p + 1)
                                own.inc_own(dve.tensor_copy(res[:, p, TOK:WIDE], att[4][:, 0:TOK]))
                        slot(unit, epilogue, before, after)
                own.leave_loop(4)
            announce(y_all, 3)
            split_y(5, xs, slice(TOK, WIDE))

            with dve.Fori(0, 4) as i:
                own.enter_loop(i, STEPS["proj"])
                for j in range(4):
                    unit = Unit(U_PROJ, i, 4, j)
                    k = 4 * i + j

                    def epilogue(zz):
                        zb = z_b[:, j % 2, :]
                        tt(zz[:, 0:TOK], zz[:, 0:TOK], zz[:, TOK:WIDE], ALU.add)
                        tt(zb[:, 0:TOK], zb[:, 0:TOK], zb[:, TOK:WIDE], ALU.add)
                        own.wait_own()
                        tt(zz[:, 0:TOK], zz[:, 0:TOK], gates[:, k, :], ALU.mult)
                        tt(zb[:, 0:TOK], zb[:, 0:TOK], gates[:, KT + k, :], ALU.mult)
                        own.wait_own()
                        return dve.tensor_tensor(res[:, k, TOK:WIDE], zz[:, 0:TOK], zb[:, 0:TOK], ALU.add)
                    slot(unit, epilogue)
                own.leave_loop(4)
            announce(y_all, 4)
            split_y(6, xs, slice(TOK, WIDE))
            layer_out(2, U_OUT2, 4, 0, False, STEPS["out2"])
            announce(rms_go, 2)
            finish_rsqrt(TOK, RMS_EPS, 3)
            normed(3, "norm_mlp_g", xs, 7, 48)

            for c in range(4):
                with dve.Fori(0, 4) as i:
                    own.enter_loop(i, STEPS["up"])
                    for j in range(4):
                        k = 4 * i + j
                        unit = Unit(U_MLP + 32 * c, i, 4, j)

                        def epilogue(zz):
                            tt(zz[:, 0:TOK], zz[:, 0:TOK], zz[:, TOK:WIDE], ALU.add)
                            own.wait_own()
                            stt(h_tmp[0][:, 0:TOK], zz[:, 0:TOK], 0.0, zz[:, 0:TOK], ALU.max, ALU.mult)
                            own.wait_own()
                            own.inc(dve.memset(tiny[:, 62:63], 0.0), h_full, 64 + 16 * c + k + 1)
                            return dve.memset(tiny[:, 61:62], 0.0)

                        def after():
                            rest_x(8 + c, k, h_tmp[0][:, 0:TOK], hidden, TOK)
                        slot(unit, epilogue, after=after)
                    own.leave_loop(4)
                if c < 3:
                    layer_out(3, U_MLP + 32 * c + 16, 4, 0, False, STEPS["out2"])
                else:
                    layer_out(3, U_MLP + 32 * c + 16, 3, 0, False, STEPS["out2"])
                    for j in range(4):
                        def epilogue(zz):
                            tt(zz[:, 0:TOK], zz[:, 0:TOK], zz[:, TOK:WIDE], ALU.add)
                            own.wait_own()
                            r = res[:, 12 + j, 0:TOK]
                            return dve.tensor_tensor(r, r, zz[:, 0:TOK], ALU.add)
                        slot(Unit(UNITS - 4, 0, 4, j), epilogue, last=j >= 2)
            announce(rms_go, 3)
            finish_rsqrt(TOK, RMS_EPS, 4)
            with dve.Fori(0, KT // 2) as i:
                own.enter_loop(i, 0)
                for b in range(2):
                    k = 2 * i + b
                    own.inc(stt_i(res[:, k, TOK:WIDE], res[:, k, 0:TOK], vcol("norm_final_g", k), rstd[:, 0:TOK],
                                     ALU.mult, ALU.mult), out_full, k + 1)
                own.leave_loop(KT // 2)

        @block.tensor
        def _(pe):
            def product(unit, mode, phase=None, operand=None):
                bank = gemm_bank[unit.slot % 2]
                for g in range(2):
                    pe.wait_ge(lo_done, 2 * unit.number + g + 1)
                    if g == 0 and (unit.exact[3] >= 2 or unit.exact[0] > 0 or not isinstance(unit.exact[1], int)):
                        pe.wait_ge(z_full, unit.number - 1)
                    n = 2 * (unit.slot % 2) + g
                    for kk in range(KT // 2):
                        k = 8 * g + kk
                        if phase is not None and kk % 4 == 0:
                            pe.wait_ge(x_full, 16 * phase + k + 4)
                        hi = w_hi[:, n, P * kk:P * (kk + 1)]
                        lo = w_lo[:, n, P * kk:P * (kk + 1)]
                        first, last = k == 0, k == KT - 1
                        if mode == "mod":
                            pe.matmul(bank[0:SQUARE, 0:P], cond_x[:, k, :], hi, start=first, stop=False)
                            ins = pe.matmul(bank[0:SQUARE, 0:P], cond_x[:, k, :], lo, start=False, stop=last)
                        elif mode == "wide":
                            pe.matmul(bank[:, :], hi, operand[:, k, 0, :], start=first, stop=False)
                            pe.matmul(bank[:, :], hi, operand[:, k, 1, :], start=False, stop=False)
                            ins = pe.matmul(bank[:, :], lo, operand[:, k, 0, :], start=False, stop=last)
                        elif mode == "pair":
                            b = bank if g == 0 else att[unit.slot % 2]
                            first, last = kk == 0, kk == KT // 2 - 1
                            pe.matmul(b[:, :].rearrange("p (a t) -> p a t", a=2), hi, operand[:, k, :, 0:TOK],
                                      start=first, stop=False)
                            ins = pe.matmul(b[:, 0:TOK], lo, operand[:, k, 0, 0:TOK], start=False, stop=last)
                        else:
                            pe.matmul(bank[:, :].rearrange("p (a t) -> p a t", a=2), hi, operand[:, k, :, 0:TOK],
                                      start=first, stop=False)
                            ins = pe.matmul(bank[:, 0:TOK], lo, operand[:, k, 0, 0:TOK], start=False, stop=last)
                    ins.then_inc(half_used, 1)

            pe.wait_ge(cond_full, 1)
            for j in range(4):
                product(Unit(0, 0, 4, j), "mod")
            with pe.Fori(0, U_IN0 // 4 - 1) as i:
                for j in range(4):
                    product(Unit(4, i, 4, j), "mod")
            pe.wait_ge(const_in, 16 * 5)

            def layer_in(l):
                n_tiles = 4 if l == 0 else 2
                with pe.Fori(0, 4 if l == 0 else 2) as i:
                    for j, kind, pair, half, wide in in_slots(l):
                        p = i if l == 0 else 2 * i + pair
                        h = 2 * p + half
                        hh = 8 * l + h
                        unit = Unit(U_IN[l], i, 28, j)
                        product(unit, "wide" if wide else "narrow", 0 if l == 0 else 2, x)
                        if kind == "v":
                            pe.wait_ge(z_used, unit.number if l == 1 else unit.number - 1)
                            for t in range(n_tiles):
                                keys = slice(0, WIDE) if t < 2 else slice(TOK, WIDE)
                                for m in range(2):
                                    rows = slice(QK * m, QK * (m + 1))
                                    o = att[2 * t + m][:, :] if t < 2 else att[4 + m][:, TOK * (t - 2):TOK * (t - 1)]
                                    ins = pe.matmul(o, q_t[rows, P * t:P * (t + 1)], k_t[rows, keys],
                                                    start=True, stop=True)
                                ins.then_inc(s_done, 1)
                        elif kind == "ag":
                            if l == 0:
                                pe.wait_ge(exp_done, tiles(l, h) + 4)
                            pe.wait_ge(z_used, unit.number if l == 1 else unit.number - 1)
                            for t in range(4):
                                ins = pe.transpose(att[5][:, P * t:P * (t + 1)], v_t[:, P * t:P * (t + 1)], ident[:])
                            ins.then_inc(vt_done, 1)
                        elif kind in ("cu", "cb"):
                            for t in range(2):
                                pe.wait_ge(a_full, tiles(l, h) + t + 1)
                                for c in range(4):
                                    ins = pe.transpose(att[t][:, P * c:P * (c + 1)], probs(t, 0)[:, P * c:P * (c + 1)],
                                                       ident[:])
                                ins.then_inc(t_done, 1)
                            if l == 0:
                                pe.wait_ge(a_full, tiles(l, h) + 4)
                                for t in range(2, 4):
                                    for c in range(2):
                                        n = 2 * (t - 2) + c
                                        ins = pe.transpose(att[2][:, P * n:P * (n + 1)], probs(t, 0)[:, P * c:P * (c + 1)],
                                                           ident[:])
                                ins.then_inc(t_done, 1)
                        elif kind in ("cc", "cg"):
                            pe.wait_ge(v_full, hh + 1)
                            pe.wait_ge(at_full, t_banks(l, h) + (3 if l == 0 else 2))
                            for t in range(n_tiles):
                                o = att[3][:, P * t:P * (t + 1)]
                                n_keys = 4 if t < 2 else 2
                                for c in range(n_keys):
                                    a = a_t[:, t, P * c:P * (c + 1)] if t < 2 else \
                                        a_t[:, 2, P * (2 * (t - 2) + c):P * (2 * (t - 2) + c + 1)]
                                    ins = pe.matmul(o, a, v_tok[:, 4 - n_keys + c, :], start=c == 0, stop=c == n_keys - 1)
                            ins.then_inc(o_done, 1)
                            if kind == "cg":
                                pe.wait_ge(pool_w_in, 64 * l + 16 * p + 16)
                                pe.wait_ge(pool_d, 4 * l + p + 1)
                                ycols = slice(0, WIDE) if l == 0 else slice(TOK, WIDE)
                                pe.matmul(att[5][:, 0:ycols.stop - ycols.start], pool_sb[:, :],
                                          res[:, 12 + p, ycols], start=True, stop=True).then_inc(pool_mm, 1)
                        elif kind in ("pu", "pg"):
                            pe.wait_ge(o_full, hh + 1)
                            for t in range(n_tiles):
                                ins = pe.transpose(att[4][:, P * t:P * (t + 1)], o_sb[:, P * t:P * (t + 1)], ident[:])
                            ins.then_inc(ot_done, 1)
                        if l == 0:
                            product(unit.ahead(1), "mod")

            def plain(begin, turns, mode, phase, operand, mods=False):
                with pe.Fori(0, turns) as i:
                    for j in range(4):
                        if mods and j % 2:
                            product(Unit(begin, i, 4, j), "mod")
                        else:
                            product(Unit(begin, i, 4, j), mode, phase, operand)

            def sum_squares(n, t):
                for k in range(KT):
                    pe.wait_ge(sq_full, 16 * n + k + 1)
                    pe.matmul(att[1][:, 0:t], mean_w[:], sq[k % 2][:, 0:t], start=k == 0, stop=k == KT - 1)\
                      .then_inc(sq_used, 1)

            def mean(l, t):
                pe.wait_ge(sum_full, l + 1)
                pe.matmul(att[0][:, 0:t], mean_w[:], total[:, 0:t], start=True, stop=True).then_inc(mu_done, 1)

            layer_in(0)
            plain(U_OUT0, 4, "wide", 1, x, mods=True)
            plain(U_OUT0 + 16, 2, "wide", 1, x)
            mean(0, WIDE)
            sum_squares(0, WIDE)
            layer_in(1)
            plain(U_OUT1, 4, "narrow", 3, x)
            mean(1, TOK)
            sum_squares(1, TOK)
            sum_squares(2, TOK)

            pe.wait_ge(f_lo, 1)
            pe.wait_ge(x_full, 16 * 5)
            for t in range(2):
                toks = slice(P * t, P * (t + 1))
                for k in range(KT):
                    o = att[3][:, HEADS * t:HEADS * (t + 1)]
                    pe.matmul(o, xs[:, k, 0, toks], wf_hi[:, k, :], start=k == 0, stop=False)
                    pe.matmul(o, xs[:, k, 0, toks], wf_lo[:, k, :], start=False, stop=False)
                    ins = pe.matmul(o, xs[:, k, 1, toks], wf_hi[:, k, :], start=False, stop=k == KT - 1)
            ins.then_inc(f_mm, 1)
            pe.wait_ge(f_full, 1)
            pe.matmul(att[4][:, 0:HEADS], table_sb[:, 4, 0:P], log_f[:, 0, :], start=True, stop=True)
            pe.matmul(att[4][:, HEADS:2 * HEADS], table_sb[:, 4, P:2 * P], log_f[:, 0, :], start=True, stop=False)
            pe.matmul(att[4][:, HEADS:2 * HEADS], table_sb[:, 4, 0:P], log_f[:, 1, :], start=False, stop=True)\
              .then_inc(f_cum, 1)

            with pe.Fori(0, 4) as i:
                for half in range(2):
                    p = 2 * i + half
                    for s, kind in enumerate(IN2_SLOTS):
                        unit = Unit(U_IN2, i, 20, 10 * half + s)
                        product(unit, "narrow", 4, xs)
                        c = int(kind == "vb")
                        if kind in ("va", "vb"):
                            pe.wait_ge(z_used, unit.number + 1)
                            if c == 1:
                                pe.wait_ge(lb_full, p + 1)
                            for t in range(2):
                                keys = P * (t + 1)
                                o = att[c][:, TOK * t:TOK * t + keys]
                                q = q_t[:, TOK * c + P * t:TOK * c + P * (t + 1)]
                                ins = pe.matmul(o, q, k_t[:, TOK * c:TOK * c + keys], start=True, stop=c == 0)
                                if c == 1:
                                    ins = pe.matmul(o, log_b[:, 0, :], table_sb[:, 4, 0:keys], start=False, stop=t == 0)
                                    if t == 1:
                                        ins = pe.matmul(att[c][:, TOK + P:2 * TOK], log_b[:, 1, :], table_sb[:, 4, 0:P],
                                                        start=False, stop=True)
                            ins.then_inc(s_done, 1)
                            for t in range(2):
                                a = TOK * c + P * t
                                ins = pe.transpose(att[5][:, P * t:P * (t + 1)], v_t[:, a:a + P], ident[:])
                            ins.then_inc(vt_done, 1)
                        elif kind in ("qb", "ga0"):
                            c = int(kind == "ga0")
                            pe.wait_ge(exp_done, TILES1 + 2 * p + c + 1)
                            for n, (t, kb) in enumerate(((0, 0), (1, 0), (1, 1))):
                                ins = pe.transpose(att[2][:, P * n:P * (n + 1)],
                                                   work[:, 2 * c + t, P * kb:P * (kb + 1)], ident[:])
                            ins.then_inc(t_done, 1)
                        elif kind in ("kb", "ga1"):
                            c = int(kind == "ga1")
                            pe.wait_ge(v_full, HEADS1 + 2 * p + c + 1)
                            pe.wait_ge(at_full, TBANKS1 + 2 * p + c + 1)
                            pe.matmul(att[3][:, 0:P], a_t[:, c, 0:P], v_tok[:, 2 * c, :], start=True, stop=True)
                            pe.matmul(att[3][:, P:2 * P], a_t[:, c, P:2 * P], v_tok[:, 2 * c, :], start=True, stop=False)
                            pe.matmul(att[3][:, P:2 * P], a_t[:, c, 2 * P:3 * P], v_tok[:, 2 * c + 1, :],
                                      start=False, stop=True).then_inc(o_done, 1)
                        if kind in ("vb", "gb0"):
                            c = int(kind == "gb0")
                            pe.wait_ge(o_full, HEADS1 + 2 * p + c + 1)
                            for t in range(2):
                                ins = pe.transpose(att[4][:, P * t:P * (t + 1)], v_out(c)[:, P * t:P * (t + 1)], ident[:])
                            ins.then_inc(ot_done, 1)

            plain(U_PROJ, 4, "pair", 5, xs)
            plain(U_OUT2, 4, "narrow", 6, xs)
            sum_squares(3, TOK)
            for c in range(4):
                plain(U_MLP + 32 * c, 4, "narrow", 7, xs)
                plain(U_MLP + 32 * c + 16, 4, "narrow", 8 + c, hidden)
            sum_squares(4, TOK)


STEPS = {"mod": 4, "in0": 95, "out0a": 8, "out0b": 12, "in1": 130, "out1": 12, "in2": 32, "proj": 16, "out2": 4, "up": 8}


def units_of(w):
    n = w.shape[1] // P
    return w.reshape(KT, P, n, P).transpose(2, 1, 0, 3).reshape(n, P, UNIT)


def columns(v):
    return np.ascontiguousarray(v).reshape(-1, P).T


def in_order(w):
    u = units_of(w)
    cu, cb, cc, cg, q, k, v, ag, pu, pg = np.split(np.arange(56), [4, 8, 12, 16, 24, 32, 40, 48, 52])
    where = {"cu": cu, "cb": cb, "cc": cc, "cg": cg, "pu": pu, "pg": pg}
    heads = {"q": q, "k": k, "v": v, "ag": ag}
    order = [heads[kind][2 * pair + half] if kind in heads else where[kind][pair]
             for pair in range(4) for kind, half in IN_SLOTS]
    return u[np.array(order)]


def weight_stream(a):
    parts = [units_of(a["w_mod"][0][:, :2 * D])]
    mods = np.concatenate([units_of(a["w_mod"][0][:, 2 * D:]), units_of(a["w_mod"][1])])
    u = in_order(a["w_in"][0])
    parts.append(np.stack([u, mods[:56]], 1).reshape(-1, P, UNIT))
    u = units_of(a["w_out"][0])
    parts.append(np.stack([u[:8], mods[56:]], 1).reshape(-1, P, UNIT))
    parts += [u[8:], in_order(a["w_in"][1]), units_of(a["w_out"][1])]
    w = a["w_in_2"]
    u = units_of(np.concatenate([w[:, :6144], w[:, 6152:]], 1))
    starts = {"qa": 0, "ka": 8, "va": 16, "qb": 24, "kb": 32, "vb": 40}
    order = []
    for p in range(HEADS):
        order += [starts[s] + p for s in IN2_SLOTS[:6]]
        order += [48 + 2 * p, 48 + 2 * p + 1, 64 + 2 * p, 64 + 2 * p + 1]
    parts.append(u[np.array(order)])
    parts.append(units_of(np.concatenate([a["w_proj_a_2"], a["w_proj_b_2"]], 0)))
    parts.append(units_of(a["w_out_2"]))
    for c in range(4):
        parts.append(units_of(a["w_up_2"][:, D * c:D * (c + 1)]))
        parts.append(units_of(a["w_down_2"][D * c:D * (c + 1)]))
    return np.concatenate(parts)


def shape_tables():
    n = QK // 4
    inv = 10000.0 ** (-np.arange(n, dtype=np.float32) / n)
    t = np.arange(TOK)
    by_row, by_col = (t // 64)[None, :] * inv[:, None], (t % 64)[None, :] * inv[:, None]
    angle = np.concatenate([by_row, by_row, by_col, by_col] * 2).astype(np.float32)
    sign = np.where(np.arange(P) % 32 < 16, -1.0, 1.0)[:, None]
    rope = np.stack([np.cos(angle), np.sin(angle) * sign], 1).astype(np.float32)
    squares = np.stack([np.eye(P), np.full((P, P), 1.0 / D)], 1).astype(np.float32)
    q, k = np.arange(P)[:, None], np.arange(TOK)[None, :]
    tables = np.zeros((P, 5, TOK), np.float32)
    for b in range(2):
        far = (q + P * b) - k
        tables[:, b] = np.where(far >= 0, -far, MASKED)
        tables[:, 2 + b] = np.where(far >= 0, 0.0, MASKED)
    tables[:, 4] = q <= k
    edge = np.zeros((4, 16), np.float32)
    for g, w in enumerate(WINDOWS):
        for e in range(16):
            tok = e if e < 8 else TOK - 16 + e
            edge[g, e] = w / (min(tok + w - w // 2, TOK) - max(tok - w // 2, 0))
    slope = 2.0 ** (-8.0 * np.arange(1, HEADS + 1) / HEADS)
    return rope, squares, tables, edge.reshape(-1), slope.astype(np.float32)


def kernel(**inputs):
    import concourse.bacc as bacc
    from concourse.bass_utils import run_bass_kernel_spmd

    a = {k: np.asarray(v) for k, v in inputs.items()}
    rope, squares, tables, edge, slope = shape_tables()

    def spread(v):
        return np.broadcast_to(v.reshape(1, -1), (P, v.size))

    vec = [columns(a["b_mod"]),
           columns(a["conv_w"]), a["subln_g"].T, columns(a["pool_scale"]), columns(a["ln_g"]), columns(a["ln_b"]),
           columns(a["norm_mix_g_2"]), columns(a["norm_mlp_g_2"]), columns(a["norm_final_g_2"]),
           spread(a["b_forget_2"]), spread(slope), spread(edge)]
    lam = np.stack([a["lam_q1"], a["lam_k1"], a["lam_q2"], a["lam_k2"]], 1)
    both = np.concatenate([a["x"][0], a["ctx"][0]], 0)
    arrays = {
        "stream": weight_stream(a),
        "tokens": both.T.reshape(KT, P, WIDE).transpose(1, 0, 2),
        "cond": np.stack([a["c"][0], a["c_ctx"]], 0).reshape(2, KT, P).transpose(2, 1, 0),
        "vectors": np.concatenate(vec, 1),
        "lam_in": spread(lam),
        "pool_w": a["pool_w"].reshape(LAYERS * 4, P, P),
        "w_forget": a["w_in_2"][:, 6144:6152].reshape(KT, P, HEADS).transpose(1, 0, 2),
        "rope": rope, "squares": squares, "tables": tables,
    }
    arrays = {k: np.ascontiguousarray(v) for k, v in arrays.items()}
    nc = bacc.Bacc("TRN2", target_bir_lowering=False, num_devices=1)
    args = [nc.dram_tensor(k, v.shape, mybir.dt.from_np(v.dtype), kind="ExternalInput").ap()
            for k, v in arrays.items()]
    out = nc.dram_tensor("out", (P, KT, TOK), F32, kind="ExternalOutput").ap()
    two_blocks(nc, *args, out)
    r = run_bass_kernel_spmd(nc, [arrays], core_ids=[0])
    y = r.results[0]["out"]
    return np.ascontiguousarray(y.transpose(2, 1, 0)).reshape(1, TOK, D)
```

```python
import math
from contextlib import ExitStack

import numpy as np

import concourse.bass as bass
from concourse import mybir

F32 = mybir.dt.float32
F32R = mybir.dt.float32r
ALU = mybir.AluOpType
ACT = mybir.ActivationFunctionType
AX = mybir.AxisListType.X

P = 128
D = 2048
TOK = 256
WIDE = 2 * TOK
KT = D // P
LAYERS = 2
HEADS = 8
QK = 64
ALPHA = (2 * LAYERS) ** 0.25
LN_EPS = 1e-5
SUB_EPS = 1e-5
RMS_EPS = 1e-6
DIFF_SCALE = QK ** -0.5
HEAD_SCALE = P ** -0.5
WINDOWS = (2, 4, 8, 16)
LAM_INIT = [0.8 - 0.6 * math.exp(-0.3 * l) for l in range(LAYERS)]
MASKED = -1e30

UNIT = KT * P
HALF = UNIT // 2
SQUARE = 32
RAW_SLOTS = 4
SPLIT_SLOTS = 4
NMOD = 3 * D // P

U_IN0 = 2 * KT
U_OUT0 = U_IN0 + 2 * 56
U_IN1 = U_OUT0 + 16 + 8
U_OUT1 = U_IN1 + 56
U_IN2 = U_OUT1 + 16
U_PROJ = U_IN2 + 80
U_OUT2 = U_PROJ + 16
U_MLP = U_OUT2 + 16
UNITS = U_MLP + 4 * 32

IN_SLOTS = [("q", 0), ("k", 0), ("v", 0), ("ag", 0), ("cu", 0), ("cc", 0), ("pu", 0),
            ("q", 1), ("k", 1), ("v", 1), ("ag", 1), ("cg", 1), ("pg", 1), ("cb", 1)]
IN2_SLOTS = ["qa", "ka", "va", "qb", "kb", "vb", "ga0", "ga1", "gb0", "gb1"]

VEC_COLS = {}
VEC_WIDTH = 0
for _name, _n in (("b_mod", LAYERS * NMOD), ("conv_w", LAYERS * 12), ("subln_g", LAYERS),
                  ("pool_scale", LAYERS * 4), ("ln_g", LAYERS * KT), ("ln_b", LAYERS * KT),
                  ("norm_mix_g", KT), ("norm_mlp_g", KT), ("norm_final_g", KT),
                  ("b_forget", 1), ("slope", HEADS), ("pool_edge", 4 * 16)):
    VEC_COLS[_name] = VEC_WIDTH
    VEC_WIDTH += _n


class InOrder:

    def __init__(self, engine, own):
        self.engine, self.own, self.base, self.count, self.last = engine, own, 0, 0, None

    def inc_own(self, instruction):
        instruction.then_inc(self.own, 1)
        self.count += 1
        self.last = (self.own, self.base + self.count)

    def inc(self, instruction, semaphore, value):
        instruction.then_inc(semaphore, 1)
        self.last = (semaphore, value)

    def wait_own(self):
        self.engine.wait_ge(*self.last)

    def enter_loop(self, i, steps):
        self.outer = (self.base, self.count, steps)
        self.base, self.count = self.base + self.count + i * steps, 0
        self.last = (self.own, self.base)

    def leave_loop(self, turns):
        base, count, steps = self.outer
        assert self.count == steps, f"the body takes {self.count} steps, not {steps}"
        self.base, self.count = base, count + turns * steps
        self.last = (self.own, self.base + self.count)


class Unit:

    def __init__(self, first, i, per, j):
        assert first % RAW_SLOTS == 0 and per % RAW_SLOTS == 0
        self.number = first + per * i + j
        self.slot = j % RAW_SLOTS
        self.wave = first // RAW_SLOTS + (per // RAW_SLOTS) * i + j // RAW_SLOTS
        self.exact = (first, i, per, j)

    def ahead(self, n):
        first, i, per, j = self.exact
        return Unit(first, i, per, j + n)


def two_blocks(nc, stream, tokens, cond, vectors, lam_in, pool_w, w_forget, rope, squares, tables, out):
    ctx = ExitStack()
    with ctx:
        at = [16512]

        def place(name, shape, dtype=F32, offset=None):
            here = at[0] if offset is None else offset
            if offset is None:
                at[0] += -(-4 * int(np.prod(shape)) // 32) * 32
                assert at[0] <= nc.sbuf_usable_end, (name, at[0] - nc.sbuf_usable_end)
            return nc.alloc_sbuf_tensor_at(name, [P, *shape], dtype, offset=here)

        def sem(name):
            return ctx.enter_context(nc.semaphore(name))

        raw = place("raw", [RAW_SLOTS, UNIT])
        w_hi = place("w_hi", [SPLIT_SLOTS, HALF], F32R)
        w_lo = place("w_lo", [SPLIT_SLOTS, HALF], F32R)
        x_at = at[0]
        x = place("x", [KT, 2, WIDE], F32R)
        xs = place("xs", [KT, 2, TOK], F32R, x_at)
        gates = place("gates", [2 * KT, TOK], F32, x_at + 4 * KT * WIDE)
        hidden = place("hidden", [KT, 2, TOK], F32R, x_at)
        mlp_x = place("mlp_x", [KT, 2, TOK], F32R, x_at + 4 * KT * WIDE)
        res = place("res", [KT, WIDE])
        z = place("z", [2, WIDE])
        q_t = place("q_t", [WIDE])
        k_t = place("k_t", [WIDE])
        v_t = place("v_t", [WIDE])
        v_tok = place("v_tok", [4, P])
        work = place("work", [6, WIDE])
        a_t = place("a_t", [3, WIDE])
        se = place("se", [WIDE])
        shared_at = at[0]
        conv_in = place("conv_in", [2, TOK + 2])
        pad_a = place("pad_a", [2, TOK + 16])
        pad_b = place("pad_b", [2, TOK + 16])
        rope_sb = place("rope_sb", [2, TOK])
        shared_end = at[0]
        ident = place("ident", [P])
        mean_w = place("mean_w", [P])
        pool_sb = place("pool_sb", [P])
        vec = place("vec", [VEC_WIDTH])
        mod = place("mod", [LAYERS * NMOD, 2])
        cond_sb = place("cond_sb", [KT, 2])
        cond_e = place("cond_e", [KT, 2])
        cond_x = place("cond_x", [KT, SQUARE], F32R)
        mod_t = place("mod_t", [SQUARE])
        tiny = place("tiny", [64])
        table_sb = place("table_sb", [5, TOK], F32, shared_at)
        wf_raw = place("wf_raw", [KT, HEADS], F32, shared_at + 5120)
        wf_hi = place("wf_hi", [KT, HEADS], F32R, shared_at + 5632)
        wf_lo = place("wf_lo", [KT, HEADS], F32R, shared_at + 6144)
        log_f = place("log_f", [2], F32, shared_at + 6656)
        cum_f = place("cum_f", [2], F32, shared_at + 6688)
        log_b = place("log_b", [2, P], F32, shared_at + 6848)
        assert shared_at + 6848 + 1024 <= shared_end

        def vcol(name, i):
            return vec[:, bass.ds(VEC_COLS[name] + i, 1)]

        lam_col = [tiny[:, 4 * l + 3:4 * l + 4] for l in range(LAYERS)]
        eps_ln, eps_rms, one = (tiny[:, 8 + n:9 + n] for n in range(3))
        top = tiny[:, 16:24]
        top_s = tiny[:, 24:32]
        sums = tiny[:, 32:40]
        inv = tiny[:, 40:48]
        o_ss = tiny[:, 48:52]
        o_rs = tiny[:, 52:56]
        power = tiny[:, 12:16]

        def probs(t, m):
            if t < 2:
                return work[:, 2 * t + m, :]
            return work[:, 4 + t - 2, TOK * m:TOK * (m + 1)]

        o_sb = work[:, 1, :]
        junk = work[:, 3, 0:P]
        sq = [work[:, 2, :], work[:, 3, :]]
        h_tmp = [work[:, 0, :], work[:, 1, :]]
        x_res = [work[:, 2, :], work[:, 3, :]]
        total = work[:, 4, :]
        rstd = work[:, 5, :]
        newton = a_t[:, 0, :]
        squared = [a_t[:, 1, :], a_t[:, 2, :]]
        total_sq = work[:, 5, :]
        mean_sb = a_t[:, 2, :]
        rms_mix = a_t[:, 2, 0:TOK]
        rms_mlp2 = work[:, 4, 0:TOK]
        log_rows = a_t[0:HEADS, 2, TOK:WIDE]
        gate_rows = a_t[0:HEADS, 0, TOK:WIDE]
        z_b = work[:, 0:2, :]

        def h_buffer(l, q, b):
            return work[:, 2 * q + b, :] if l == 0 else work[:, b, TOK * q:TOK * (q + 1)]

        banks = [ctx.enter_context(nc.psum_tensor(f"bank{n}", [P, WIDE], F32)) for n in range(8)]
        gemm_bank, att = banks[0:2], banks[2:8]

        raw_full = [sem(f"raw_full{n}") for n in range(RAW_SLOTS)]
        hi_done = sem("hi_done")
        lo_done = sem("lo_done")
        half_used = sem("half_used")
        z_full = sem("z_full")
        z_used = sem("z_used")
        z_sum = sem("z_sum")
        se_full = sem("se_full")
        h_full = sem("h_full")
        xhi_done = sem("xhi_done")
        x_full = sem("x_full")
        y_all = sem("y_all")
        s_done = sem("s_done")
        top_done = sem("top_done")
        exp_done = sem("exp_done")
        a_full = sem("a_full")
        t_done = sem("t_done")
        at_full = sem("at_full")
        vt_done = sem("vt_done")
        v_full = sem("v_full")
        o_done = sem("o_done")
        ss_full = sem("ss_full")
        rs_full = sem("rs_full")
        o_full = sem("o_full")
        ot_done = sem("ot_done")
        pool_d = sem("pool_d")
        pool_mm = sem("pool_mm")
        pool_w_in = sem("pool_w_in")
        xres_in = [sem(f"xres_in{n}") for n in range(2)]
        pivot_done = sem("pivot_done")
        sum_full = sem("sum_full")
        mu_done = sem("mu_done")
        var_full = sem("var_full")
        cen_done = sem("cen_done")
        csq_full = sem("csq_full")
        csq_used = sem("csq_used")
        sq_full = sem("sq_full")
        sq_used = sem("sq_used")
        lnx_done = sem("lnx_done")
        scaled = sem("scaled")
        mean_full = sem("mean_full")
        minus_mean = sem("minus_mean")
        odd_full = sem("odd_full")
        ms_done = sem("ms_done")
        cond_in, vec_in, const_in, tok_in, table_in = (sem(n) for n in ("cond_in", "vec_in", "const_in", "tok_in", "table_in"))
        cond_exp = sem("cond_exp")
        cond_hi = sem("cond_hi")
        cond_silu = sem("cond_silu")
        cond_full = sem("cond_full")
        lam_sum = sem("lam_sum")
        lam_exp = sem("lam_exp")
        f_hi = sem("f_hi")
        f_lo = sem("f_lo")
        f_mm = sem("f_mm")
        f_in = sem("f_in")
        f_exp = sem("f_exp")
        f_full = sem("f_full")
        lf_done = sem("lf_done")
        lb_full = sem("lb_full")
        f_cum = sem("f_cum")
        out_full = sem("out_full")
        out_in = sem("out_in")
        act_own, dve_own, pool_own = sem("act_own"), sem("dve_own"), sem("pool_own")

        def tiles(l, h):
            return 4 * h if l == 0 else 4 * HEADS + 2 * h

        def t_banks(l, h):
            return 3 * h if l == 0 else 3 * HEADS + 2 * h

        HEADS1 = LAYERS * HEADS
        TILES1 = tiles(1, HEADS)
        TBANKS1 = t_banks(1, HEADS)
        U_IN = [U_IN0, U_IN1]

        def in_slots(l):
            found = []
            for pair in range(1 if l == 0 else 2):
                for s, (kind, half) in enumerate(IN_SLOTS):
                    j = 2 * s if l == 0 else 14 * pair + s
                    found.append((j, kind, pair, half, l == 0 or kind in "kv"))
            return found

        block = ctx.enter_context(nc.Block())

        @block.sync
        def _(sp):
            def load(unit, waits=True):
                if waits:
                    sp.wait_ge(lo_done, 2 * (unit.number - RAW_SLOTS) + 2)
                sp.dma_start(raw[:, unit.slot, :], stream[unit.number]).then_inc(raw_full[unit.slot], 16)

            for j in range(RAW_SLOTS):
                load(Unit(0, 0, 4, j), waits=False)
            with sp.Fori(0, UNITS // RAW_SLOTS - 1) as i:
                for j in range(RAW_SLOTS):
                    load(Unit(RAW_SLOTS, i, RAW_SLOTS, j))
            with sp.Fori(0, KT // 2) as i:
                for b in range(2):
                    sp.wait_ge(out_full, 2 * i + b + 1)
                    sp.dma_start(out[:, 2 * i + b, :], res[:, 2 * i + b, TOK:WIDE]).then_inc(out_in, 16)
            sp.wait_ge(out_in, 16 * KT)

        @block.gpsimd
        def _(pool):
            own = InOrder(pool, pool_own)
            own.inc_own(pool.memset(pad_a[:], 0.0))

            def windows(l, g):
                n = 2 if l == 0 else 1
                done = 4 * l + g
                if done:
                    pool.wait_ge(pool_mm, done)
                pool.dma_start(pool_sb[:, :], pool_w[4 * l + g]).then_inc(pool_w_in, 16)
                j = 28 * g + 12 if l == 0 else 14 * g + 6
                pool.wait_ge(z_used, U_IN[l] + j + 1)
                row = res[:, 4 * g + 3, (0 if l == 0 else TOK):WIDE].rearrange("p (n t) -> p n t", t=TOK)
                own.wait_own()
                for edge in (slice(0, 8), slice(TOK + 8, TOK + 16)):
                    own.inc_own(pool.memset(pad_a[:, 0:n, edge], 0.0))
                own.inc_own(pool.tensor_copy(pad_a[:, 0:n, 8:8 + TOK], row))
                src, dst = pad_a, pad_b
                lo, hi = 1, TOK + 16
                own.wait_own()
                own.inc_own(pool.tensor_tensor(dst[:, 0:n, lo:hi], src[:, 0:n, lo - 1:hi - 1], src[:, 0:n, lo:hi], ALU.add))
                for level in range(1, g + 1):
                    d = 1 << (level - 1)
                    src, dst = dst, src
                    lo, hi = lo + d, hi - d
                    own.wait_own()
                    own.inc_own(pool.tensor_tensor(dst[:, 0:n, lo:hi], src[:, 0:n, lo - d:hi - d],
                                                src[:, 0:n, lo + d:hi + d], ALU.add))
                assert lo <= 8 and hi >= 8 + TOK
                own.wait_own()
                own.inc_own(pool.tensor_scalar(dst[:, 0:n, 8:8 + TOK], dst[:, 0:n, 8:8 + TOK],
                                            1.0 / WINDOWS[g], 1.0, ALU.mult, ALU.mult))
                own.wait_own()
                for s in range(n):
                    for e, c in ((0, 8), (8, TOK)):
                        edge = vec[:, VEC_COLS["pool_edge"] + 16 * g + e:VEC_COLS["pool_edge"] + 16 * g + e + 8]
                        own.inc_own(pool.tensor_tensor(dst[:, s, c:c + 8], dst[:, s, c:c + 8], edge, ALU.mult))
                own.wait_own()
                own.inc(pool.tensor_tensor(row, dst[:, 0:n, 8:8 + TOK], row, ALU.subtract), pool_d, done + 1)

            def root(l, h):
                n = 4 if l == 0 else 2
                pool.wait_ge(ss_full, 8 * l + h + 1)
                own.inc_own(pool.tensor_scalar(o_ss[:, 0:n], o_ss[:, 0:n], 1.0 / P, SUB_EPS, ALU.mult, ALU.add))
                own.wait_own()
                own.inc(pool.tensor_tensor(o_rs[:, 0:n], o_ss[:, 0:n], power[:, 0:n], ALU.pow),
                        rs_full, 8 * l + h + 1)

            def mixers(l):
                for p in range(HEADS // 2):
                    root(l, 2 * p)
                    windows(l, p)
                    root(l, 2 * p + 1)

            own.inc_own(pool.memset(power, -0.5))
            pool.dma_start(res[:, 0:2, :], tokens[:, 0:2, :]).then_inc(tok_in, 16)
            with pool.Fori(0, KT // 2 - 1) as i:
                own.enter_loop(i, 0)
                pool.wait_ge(tok_in, 16 * i + 16)
                ahead = bass.ds(2 * i + 2, 2)
                pool.dma_start(res[:, ahead, :], tokens[:, ahead, :]).then_inc(tok_in, 16)
                own.leave_loop(KT // 2 - 1)
            pool.wait_ge(vec_in, 16)
            mixers(0)
            for b in range(2):
                if b == 0:
                    pool.wait_ge(z_used, U_OUT0)
                    pool.wait_ge(o_full, HEADS)
                pool.dma_start(x_res[b], tokens[:, b, :]).then_inc(xres_in[b], 16)
            with pool.Fori(0, 3) as i:
                for b in range(2):
                    pool.wait_ge(z_used, U_OUT0 + 4 * i + 2 * b + 1)
                    pool.dma_start(x_res[b], tokens[:, 2 * i + b + 2, :]).then_inc(xres_in[b], 16)
            for b in range(2):
                pool.wait_ge(z_used, U_OUT0 + 12 + 2 * b + 1)
                pool.dma_start(x_res[b], tokens[:, 8 + b, :]).then_inc(xres_in[b], 16)
            with pool.Fori(0, 3) as i:
                for b in range(2):
                    pool.wait_ge(z_used, U_OUT0 + 16 + 2 * i + b + 1)
                    pool.dma_start(x_res[b], tokens[:, 2 * i + b + 10, :]).then_inc(xres_in[b], 16)
            def subtract_mean(l):
                t = WIDE if l == 0 else TOK
                pool.wait_ge(mean_full, l + 1)
                with pool.Fori(0, KT - 4) as i:
                    own.enter_loop(i, 0)
                    r = res[:, i + 4, 0:t]
                    pool.tensor_tensor(r, r, mean_sb[:, 0:t], ALU.subtract).then_inc(minus_mean, 1)
                    own.leave_loop(KT - 4)

            subtract_mean(0)
            mixers(1)
            subtract_mean(1)

        @block.scalar
        def _(act):
            own = InOrder(act, act_own)
            act.dma_start(cond_sb[:], cond).then_inc(cond_in, 16)
            act.dma_start(vec[:], vectors).then_inc(vec_in, 16)
            act.dma_start(ident[:], squares[:, 0]).then_inc(const_in, 16)
            act.dma_start(work[:, 4, :], lam_in).then_inc(const_in, 16)
            act.dma_start(rope_sb[:], rope).then_inc(const_in, 16)
            act.dma_start(mean_w[:], squares[:, 1]).then_inc(const_in, 16)

            def round_half(unit, g):
                if g == 0:
                    act.wait_ge(raw_full[unit.slot], 16 * (unit.wave + 1))
                if unit.exact[3] >= 2 or unit.exact[0] > 0 or not isinstance(unit.exact[1], int):
                    act.wait_ge(half_used, 2 * unit.number + g + 1 - SPLIT_SLOTS)
                own.inc(act.activation(w_hi[:, 2 * (unit.slot % 2) + g, :],
                                          raw[:, unit.slot, g * HALF:(g + 1) * HALF], ACT.Copy),
                           hi_done, 2 * unit.number + g + 1)

            def take(unit, width=WIDE):
                act.wait_ge(half_used, 2 * unit.number + 2)
                if unit.exact[3] >= 2 or unit.exact[0] > 0 or not isinstance(unit.exact[1], int):
                    act.wait_ge(z_used, unit.number - 1)
                b = unit.slot % 2
                rows = SQUARE if width == P else P
                own.inc(act.activation(z[0:rows, b, 0:width], gemm_bank[b][0:rows, 0:width], ACT.Copy),
                           z_full, unit.number + 1)

            def slot(unit, width=WIDE, gate=None, wide=True, after=None, last=False):
                if not last:
                    round_half(unit.ahead(2), 0)
                take(unit, width)
                if gate is not None:
                    if wide:
                        own.wait_own()
                    else:
                        act.wait_ge(z_sum, gate - 16 + 1)
                    t = WIDE if wide else TOK
                    own.inc(act.activation(se[:, 0:t], z[:, unit.slot % 2, 0:t], ACT.Exp, scale=-1.0),
                               se_full, gate + 1)
                if not last:
                    round_half(unit.ahead(2), 1)
                if after:
                    after()

            def round_first(k, b, loaded, reuse=True):
                act.wait_ge(tok_in, 16 * loaded)
                if reuse:
                    act.wait_ge(x_full, k)
                act.wait_ge(z_used, 2 * k + 2)
                for s in range(2):
                    cols = slice(TOK * s, TOK * (s + 1))
                    last = act.activation(h_tmp[b][:, cols], res[:, k, cols], ACT.Identity,
                                          scale=mod[:, KT + k, s:s + 1], bias=mod[:, k, s:s + 1])
                own.inc(last, h_full, k + 1)
                own.wait_own()
                act.activation(x[:, k, 0, :], h_tmp[b], ACT.Copy).then_inc(xhi_done, 1)

            act.wait_ge(cond_in, 16)
            act.activation(cond_e[:], cond_sb[:], ACT.Exp, scale=-1.0).then_inc(cond_exp, 1)
            round_half(Unit(0, 0, 4, 0), 0)
            act.wait_ge(cond_silu, 1)
            act.activation(cond_x[:, :, 0:2], cond_sb[:], ACT.Copy).then_inc(cond_hi, 1)
            round_half(Unit(0, 0, 4, 0), 1)
            round_half(Unit(0, 0, 4, 1), 0)
            round_half(Unit(0, 0, 4, 1), 1)
            for j in range(4):
                slot(Unit(0, 0, 4, j), width=P)
            round_first(0, 0, 1, reuse=False)
            with act.Fori(0, U_IN0 // 4 - 1) as i:
                own.enter_loop(i, 0)
                for j in range(4):
                    slot(Unit(4, i, 4, j), width=P)
                    if j == 1:
                        round_first(2 * i + 1, 1, i + 1)
                    elif j == 3:
                        round_first(2 * i + 2, 0, i + 2)
                own.leave_loop(U_IN0 // 4 - 1)
            round_first(KT - 1, 1, KT // 2)
            act.wait_ge(lam_sum, 1)
            for l in range(LAYERS):
                last = act.activation(tiny[:, 4 * l:4 * l + 2], tiny[:, 4 * l:4 * l + 2], ACT.Exp)
            last.then_inc(lam_exp, 1)

            def softmax(count, t_list):
                for n, t in enumerate(t_list):
                    act.wait_ge(top_done, count + n + 1)
                    for m in range(2):
                        last = act.activation(probs(t, m), scores(t, m), ACT.Exp, bias=top_s[:, 2 * t + m:2 * t + m + 1],
                                              scale=DIFF_SCALE, accum_out=sums[:, 2 * t + m:2 * t + m + 1])
                    own.inc(last, exp_done, count + n + 1)

            def scores(t, m):
                return att[2 * t + m][:, :] if t < 2 else att[4 + m][:, TOK * (t - 2):TOK * (t - 1)]

            def layer_in(l):
                n_tiles = 4 if l == 0 else 2
                steps = 6 if l == 0 else 4

                with act.Fori(0, 4 if l == 0 else 2) as i:
                    own.enter_loop(i, steps)
                    for j, kind, pair, half, wide in in_slots(l):
                        p = i if l == 0 else 2 * i + pair
                        h = 2 * p + half
                        unit = Unit(U_IN[l], i, 28, j)
                        gate = {"ag": half, "cg": 2, "pg": 3}.get(kind)
                        if gate is not None:
                            gate = 16 * l + 4 * p + gate

                        def after():
                            if kind == "v":
                                softmax(tiles(l, h), range(n_tiles))
                            elif kind == "ag":
                                act.wait_ge(vt_done, 8 * l + h + 1)
                                own.inc(act.activation(v_tok[:].rearrange("p a b -> p (a b)"), att[5][:, :], ACT.Copy),
                                           v_full, 8 * l + h + 1)
                            elif kind in ("cu", "cg"):
                                n = 3 if l == 0 else 2
                                for c in range(n):
                                    act.wait_ge(t_done, t_banks(l, h) + c + 1)
                                    own.inc(act.activation(a_t[:, c, :], att[c][:, :], ACT.Copy),
                                               at_full, t_banks(l, h) + c + 1)
                            elif kind in ("cc", "pg"):
                                act.wait_ge(o_done, 8 * l + h + 1)
                                for t in range(n_tiles):
                                    if t:
                                        own.wait_own()
                                    squares = act.activation(junk, att[3][:, P * t:P * (t + 1)], ACT.Square,
                                                             accum_out=o_ss[:, t:t + 1])
                                    if t < n_tiles - 1:
                                        own.inc_own(squares)
                                own.inc(squares, ss_full, 8 * l + h + 1)
                        slot(unit, gate=gate, wide=wide, after=after)
                        if l == 0:
                            slot(unit.ahead(1), width=P)
                    own.leave_loop(4 if l == 0 else 2)

            def rough_rsqrt(t, eps, n, variance, ready, value):
                act.activation(tiny[:, 61:62], one, ACT.Ln)
                act.wait_ge(ready, value)
                own.inc_own(act.activation(rstd[:, 0:t], variance[:, 0:t], ACT.Ln, bias=eps))
                own.wait_own()
                own.inc(act.activation(rstd[:, 0:t], rstd[:, 0:t], ACT.Exp, scale=-0.5), lnx_done, n + 1)

            def square(l, k, b, unit=None):
                t = WIDE if l == 0 else TOK
                if unit is None:
                    act.wait_ge(cen_done, 16 * l + k + 1)
                else:
                    act.wait_ge(z_used, unit.number + 1)
                if not isinstance(k, int):
                    act.wait_ge(csq_used, 16 * l + k - (1 if l else 0))
                elif l or k >= 2:
                    act.wait_ge(csq_used, 16 * l + k - 1)
                act.activation(squared[b][:, 0:t], res[:, k, 0:t], ACT.Square).then_inc(csq_full, 1)

            def plain_out(begin, turns):
                with act.Fori(0, turns) as i:
                    own.enter_loop(i, 0)
                    for j in range(4):
                        slot(Unit(begin, i, 4, j))
                    own.leave_loop(turns)

            def layer_out(l, begin, turns, k0, mods=False):
                with act.Fori(0, turns) as i:
                    own.enter_loop(i, 0)
                    for j in range(4):
                        if mods and j % 2:
                            slot(Unit(begin, i, 4, j), width=P)
                            continue
                        slot(Unit(begin, i, 4, j))
                        n = j // 2 if mods else j
                        square(l, k0 + (2 * i if mods else 4 * i) + n - 1, (n + 1) % 2)
                    own.leave_loop(turns)

            def norm(l, t):
                square(l, KT - 1, 1)
                rough_rsqrt(t, eps_ln, l, a_t[:, 1, :], var_full, l + 1)
                with act.Fori(0, KT // 4) as i:
                    own.enter_loop(i, 4 if l == 0 else 0)
                    for n in range(4):
                        b, k = n % 2, 4 * i + n
                        h = h_buffer(l, n // 2, b)
                        if l == 1:
                            act.wait_ge(h_full, 16 + k + 1)
                            act.activation(xs[:, k, 0, :], h, ACT.Copy).then_inc(xhi_done, 1)
                            act.wait_ge(sq_used, 4 * i + 2 * (n // 2) + 1)
                            act.activation(sq[b][:, 0:TOK], res[:, k, 0:TOK], ACT.Square).then_inc(sq_full, 1)
                            continue
                        if b == 0:
                            act.wait_ge(scaled, k + 1)
                            act.wait_ge(x_full, 32 + k - 3)
                            for s in range(2):
                                cols = slice(TOK * s, TOK * (s + 1))
                                own.inc_own(act.activation(h[:, cols], res[:, k, cols], ACT.Identity,
                                                           scale=mod[:, NMOD + KT + k, s:s + 1],
                                                           bias=mod[:, NMOD + k, s:s + 1]))
                            own.wait_own()
                        else:
                            act.wait_ge(odd_full, 2 * i + n // 2 + 1)
                        act.activation(x[:, k, 0, :], h, ACT.Copy).then_inc(xhi_done, 1)
                    own.leave_loop(KT // 4)

            def split_y(target, cols, unit_before, early, announced=None):
                act.wait_ge(half_used, 2 * unit_before)
                act.wait_ge(lo_done, 2 * unit_before + 2)
                t = cols.stop - cols.start

                def tile(k):
                    act.activation(target[:, k, 0, 0:t], res[:, k, cols], ACT.Copy).then_inc(xhi_done, 1)
                with act.Fori(0, early // 4) as i:
                    own.enter_loop(i, 0)
                    for j in range(4):
                        tile(4 * i + j)
                    own.leave_loop(early // 4)
                if early < KT:
                    act.wait_ge(y_all, announced)
                for k in range(early, KT):
                    tile(k)

            layer_in(0)
            split_y(x, slice(0, WIDE), U_OUT0, 12, 1)
            for j in range(4):
                slot(Unit(U_OUT0, 0, 4, j), width=P if j % 2 else WIDE)
            square(0, 0, 0)
            layer_out(0, U_OUT0 + 4, 3, 2, mods=True)
            layer_out(0, U_OUT0 + 16, 2, 8)
            norm(0, WIDE)
            layer_in(1)
            split_y(x, slice(TOK, WIDE), U_OUT1, 12, 2)
            act.dma_start(table_sb[:], tables).then_inc(table_in, 16)
            act.dma_start(wf_raw[:], w_forget).then_inc(table_in, 16)
            for j in range(4):
                slot(Unit(U_OUT1, 0, 4, j))
            for k in range(3):
                square(1, k, k % 2)
            layer_out(1, U_OUT1 + 4, 3, 4)
            act.wait_ge(table_in, 32)
            act.activation(wf_hi[:], wf_raw[:], ACT.Copy).then_inc(f_hi, 1)
            norm(1, TOK)

            rough_rsqrt(TOK, eps_rms, 2, att[1], sq_used, KT + 1)
            act.wait_ge(f_in, 1)
            own.inc_own(act.activation(gate_rows, gate_rows, ACT.Exp, scale=-1.0))
            own.wait_own()
            own.inc(act.activation(gate_rows, gate_rows, ACT.Ln, bias=one[0:HEADS, :]), f_exp, 1)

            def softmax2(p, kind):
                count = TILES1 + 2 * p + kind
                act.wait_ge(top_done, count + 1)
                for t in range(2):
                    keys = P * (t + 1)
                    last = act.activation(work[:, 2 * kind + t, 0:keys], work[:, 2 * kind + t, 0:keys], ACT.Exp,
                                          bias=top_s[:, 2 * kind + t:2 * kind + t + 1], scale=HEAD_SCALE,
                                          accum_out=sums[:, 2 * kind + t:2 * kind + t + 1])
                own.inc(last, exp_done, count + 1)

            with act.Fori(0, 4) as i:
                own.enter_loop(i, 0)
                for half in range(2):
                    p = 2 * i + half
                    for s, kind in enumerate(IN2_SLOTS):
                        unit = Unit(U_IN2, i, 20, 10 * half + s)

                        def after():
                            if kind in ("va", "vb"):
                                softmax2(p, int(kind == "vb"))
                            elif kind in ("qb", "ga0"):
                                c = kind == "ga0"
                                act.wait_ge(vt_done, HEADS1 + 2 * p + c + 1)
                                own.inc(act.activation(v_tok[:, 2 * c:2 * c + 2, :].rearrange("p a b -> p (a b)"),
                                                          att[5][:, 0:2 * P], ACT.Copy), v_full, HEADS1 + 2 * p + c + 1)
                            elif kind in ("kb", "ga1"):
                                c = kind == "ga1"
                                act.wait_ge(t_done, TBANKS1 + 2 * p + c + 1)
                                own.inc(act.activation(a_t[:, c, 0:3 * P], att[2][:, 0:3 * P], ACT.Copy),
                                           at_full, TBANKS1 + 2 * p + c + 1)
                        gate = 32 + 4 * p + s - 6 if s >= 6 else None
                        slot(unit, gate=gate, wide=False, after=after)
                own.leave_loop(4)

            split_y(xs, slice(TOK, WIDE), U_PROJ, 16)
            with act.Fori(0, 4) as i:
                own.enter_loop(i, 0)
                for j in range(4):
                    unit = Unit(U_PROJ, i, 4, j)
                    round_half(unit.ahead(2), 0)
                    act.wait_ge(half_used, 2 * unit.number + 2)
                    act.wait_ge(z_used, unit.number - 1)
                    act.activation(z_b[:, j % 2, :], att[j % 2][:, :], ACT.Copy)
                    own.inc(act.activation(z[:, j % 2, :], gemm_bank[j % 2][:, :], ACT.Copy),
                               z_full, unit.number + 1)
                    round_half(unit.ahead(2), 1)
                own.leave_loop(4)
            split_y(xs, slice(TOK, WIDE), U_OUT2, 12, 3)
            with act.Fori(0, 4) as i:
                own.enter_loop(i, 0)
                for j in range(4):
                    unit = Unit(U_OUT2, i, 4, j)
                    k = 4 * i + j

                    def after():
                        act.wait_ge(h_full, 32 + k + 1)
                        act.activation(mlp_x[:, k, 0, :], h_tmp[j % 2][:, 0:TOK], ACT.Copy).then_inc(xhi_done, 1)
                        square(2, k, j % 2, unit)
                    slot(unit, after=after)
                own.leave_loop(4)
            rough_rsqrt(TOK, eps_rms, 3, att[1], ms_done, 1)

            def up(first, c):
                with act.Fori(0, 4) as i:
                    own.enter_loop(i, 0)
                    for j in range(4):
                        unit = Unit(first, i, 4, j)
                        k = 4 * i + j

                        def after():
                            act.wait_ge(h_full, 48 + 16 * c + k + 1)
                            act.activation(hidden[:, k, 0, :], h_tmp[0][:, 0:TOK], ACT.Copy).then_inc(xhi_done, 1)
                        slot(unit, after=after)
                    own.leave_loop(4)

            for c in range(4):
                up(U_MLP + 32 * c, c)
                if c < 3:
                    plain_out(U_MLP + 32 * c + 16, 4)
                else:
                    down = U_MLP + 32 * c + 16
                    with act.Fori(0, 3) as i:
                        own.enter_loop(i, 0)
                        for j in range(4):
                            unit = Unit(down, i, 4, j)
                            slot(unit, after=lambda: square(3, 4 * i + j, j % 2, unit))
                        own.leave_loop(3)
                    for j in range(4):
                        unit = Unit(UNITS - 4, 0, 4, j)
                        slot(unit, last=j >= 2, after=lambda: square(3, 12 + j, j % 2, unit))
            rough_rsqrt(TOK, eps_rms, 4, att[1], ms_done, 2)

        @block.vector
        def _(dve):
            own = InOrder(dve, dve_own)

            def tt(o, a, b, op):
                own.inc_own(dve.tensor_tensor(o, a, b, op))

            def ts(o, a, s1, op0, s2=None, op1=None):
                if op1 is None:
                    own.inc_own(dve.tensor_scalar(o, a, s1, None, op0))
                else:
                    own.inc_own(dve.tensor_scalar(o, a, s1, s2, op0, op1))

            def stt(o, a, s, b, op0, op1):
                own.inc_own(dve.scalar_tensor_tensor(out=o, in0=a, scalar=s, in1=b, op0=op0, op1=op1))

            def fence():
                own.inc_own(dve.memset(tiny[:, 60:61], 0.0))
                own.wait_own()

            def announce(semaphore, value):
                fence()
                own.inc(dve.memset(tiny[:, 62:63], 0.0), semaphore, value)
                own.wait_own()

            def rest_half(unit, g):
                dve.wait_ge(hi_done, 2 * unit.number + g + 1)
                n = 2 * (unit.slot % 2) + g
                own.inc(dve.tensor_tensor(w_lo[:, n, :], raw[:, unit.slot, g * HALF:(g + 1) * HALF],
                                             w_hi[:, n, :].bitcast(F32), ALU.subtract),
                           lo_done, 2 * unit.number + g + 1)

            def slot(unit, epilogue, before=None, after=None, last=False):
                if not last:
                    rest_half(unit.ahead(2), 0)
                if before:
                    before()
                dve.wait_ge(z_full, unit.number + 1)
                own.wait_own()
                own.inc(epilogue(z[:, unit.slot % 2, :]), z_used, unit.number + 1)
                if after:
                    after()
                if not last:
                    rest_half(unit.ahead(2), 1)

            def stt_i(o, a, s, b, op0, op1):
                return dve.scalar_tensor_tensor(out=o, in0=a, scalar=s, in1=b, op0=op0, op1=op1)

            dve.memset(conv_in[:], 0.0)
            dve.memset(cond_x[:].bitcast(F32), 0.0)
            dve.memset(eps_ln, LN_EPS)
            dve.memset(eps_rms, RMS_EPS)
            own.inc_own(dve.memset(one, 1.0))
            dve.wait_ge(cond_exp, 1)
            ts(cond_e[:], cond_e[:], 1.0, ALU.add)
            own.wait_own()
            own.inc_own(dve.reciprocal(cond_e[:], cond_e[:]))
            own.wait_own()
            own.inc(dve.tensor_tensor(cond_sb[:], cond_sb[:], cond_e[:], ALU.mult), cond_silu, 1)
            dve.wait_ge(cond_hi, 1)
            own.inc(dve.tensor_tensor(cond_x[:, :, 2:4], cond_sb[:], cond_x[:, :, 0:2].bitcast(F32), ALU.subtract),
                       cond_full, 1)
            for g in range(2):
                rest_half(Unit(0, 0, 4, 0), g)
            for g in range(2):
                rest_half(Unit(0, 0, 4, 1), g)
            dve.wait_ge(vec_in, 16)
            for l in range(LAYERS):
                scales = VEC_COLS["b_mod"] + NMOD * l + KT
                ts(vec[:, scales:scales + KT], vec[:, scales:scales + KT], 1.0, ALU.add)
            own.wait_own()
            def modulation(m):
                def epilogue(zz):
                    for c in range(P // SQUARE):
                        rows = slice(SQUARE * c, SQUARE * (c + 1))
                        last = dve.transpose(mod_t[rows, :], zz[0:SQUARE, rows])
                    own.inc_own(last)
                    own.wait_own()
                    return stt_i(mod[:, m, :], mod_t[:, 0:2], vcol("b_mod", m), mod_t[:, 2:4], ALU.add, ALU.add)
                return epilogue

            def rest_x(n, k, source, target, t):
                dve.wait_ge(xhi_done, 16 * n + k + 1)
                own.inc(dve.tensor_tensor(target[:, k, 1, 0:t], source, target[:, k, 0, 0:t].bitcast(F32),
                                             ALU.subtract), x_full, 16 * n + k + 1)

            def split_y(n, target, cols):
                with dve.Fori(0, KT // 4) as i:
                    own.enter_loop(i, 0)
                    for j in range(4):
                        k = 4 * i + j
                        rest_x(n, k, res[:, k, cols], target, cols.stop - cols.start)
                    own.leave_loop(KT // 4)

            for j in range(4):
                slot(Unit(0, 0, 4, j), modulation(j // 2 + KT * (j % 2)))
            rest_x(0, 0, h_tmp[0], x, WIDE)
            with dve.Fori(0, U_IN0 // 4 - 1) as i:
                own.enter_loop(i, STEPS["mod"])
                for j in range(4):
                    slot(Unit(4, i, 4, j), modulation(2 * i + 2 + j // 2 + KT * (j % 2)))
                    if j % 2:
                        rest_x(0, 2 * i + 1 + j // 2, h_tmp[1 - j // 2], x, WIDE)
                own.leave_loop(U_IN0 // 4 - 1)
            rest_x(0, KT - 1, h_tmp[1], x, WIDE)

            dve.wait_ge(const_in, 16 * 4)
            lam_v = work[:, 4, :].rearrange("p (l v d) -> p l v d", l=LAYERS, v=4)
            for l in range(LAYERS):
                for m in range(2):
                    n = 2 * l + m
                    tt(work[:, 5, 64 * n:64 * n + 64], lam_v[:, l, 2 * m, :], lam_v[:, l, 2 * m + 1, :], ALU.mult)
            own.wait_own()
            for l in range(LAYERS):
                last = dve.reduce_sum(tiny[:, 4 * l:4 * l + 2],
                                      work[:, 5, 128 * l:128 * l + 128].rearrange("p (m d) -> p m d", m=2), axis=AX)
            own.inc(last, lam_sum, 1)
            dve.wait_ge(lam_exp, 1)
            for l in range(LAYERS):
                tt(tiny[:, 4 * l + 2:4 * l + 3], tiny[:, 4 * l + 1:4 * l + 2], tiny[:, 4 * l:4 * l + 1], ALU.subtract)
                own.wait_own()
                ts(tiny[:, 4 * l + 3:4 * l + 4], tiny[:, 4 * l + 2:4 * l + 3], -LAM_INIT[l], ALU.add)
                ts(vcol("subln_g", l), vcol("subln_g", l), 1.0 - LAM_INIT[l], ALU.mult)

            def scores(t, m):
                return att[2 * t + m][:, :] if t < 2 else att[4 + m][:, TOK * (t - 2):TOK * (t - 1)]

            def layer_in(l, steps):
                n_tiles = 4 if l == 0 else 2
                ycols = slice(0, WIDE) if l == 0 else slice(TOK, WIDE)
                t_y = ycols.stop - ycols.start
                nseq = t_y // TOK

                def seq(ap):
                    return ap.rearrange("p (n t) -> p n t", t=TOK)

                with dve.Fori(0, 4 if l == 0 else 2) as i:
                    own.enter_loop(i, steps)
                    for j, kind, pair, half, wide in in_slots(l):
                        p = i if l == 0 else 2 * i + pair
                        h = 2 * p + half
                        hh = 8 * l + h
                        unit = Unit(U_IN[l], i, 28, j)
                        gate = {"ag": half, "cg": 2, "pg": 3}.get(kind)
                        if gate is not None:
                            gate = 16 * l + 4 * p + gate

                        def silu(zz):
                            dve.wait_ge(se_full, gate + 1)
                            ts(se[:, 0:t_y], se[:, 0:t_y], 1.0, ALU.add)
                            own.wait_own()
                            own.inc_own(dve.reciprocal(se[:, 0:t_y], se[:, 0:t_y]))
                            own.wait_own()

                        def epilogue(zz):
                            if not wide:
                                ins = dve.tensor_tensor(zz[:, 0:TOK], zz[:, 0:TOK], zz[:, TOK:WIDE], ALU.add)
                                if gate is None:
                                    own.inc_own(ins)
                                else:
                                    own.inc(ins, z_sum, gate - 16 + 1)
                                own.wait_own()
                            zt = zz[:, 0:t_y]
                            if kind in ("q", "k"):
                                dst = q_t if kind == "q" else k_t
                                tt(dst[:, 0:TOK], zz[:, 0:TOK], rope_sb[:, 0, :], ALU.mult)
                                own.inc_own(dve.stream_shuffle(se[:, 0:TOK], zz[:, 0:TOK],
                                                            [(n + 16) % 32 for n in range(32)]))
                                if wide:
                                    own.inc_own(dve.tensor_copy(dst[:, TOK:WIDE], zz[:, TOK:WIDE]))
                                own.wait_own()
                                tt(se[:, 0:TOK], se[:, 0:TOK], rope_sb[:, 1, :], ALU.mult)
                                own.wait_own()
                                return dve.tensor_tensor(dst[:, 0:TOK], dst[:, 0:TOK], se[:, 0:TOK], ALU.add)
                            if kind == "v":
                                return dve.tensor_copy(v_t[:, :], zz)
                            if kind == "ag":
                                silu(zt)
                                return stt_i(res[:, 4 * p + half, ycols], se[:, 0:t_y], vcol("subln_g", l), zt, ALU.mult, ALU.mult)
                            if kind == "cu":
                                return dve.tensor_copy(res[:, 4 * p + 2, ycols], zt)
                            y = res[:, 4 * p + 2, ycols]
                            if kind == "cc":
                                tt(conv_in[:, 0:nseq, 1:TOK + 1], seq(zt), seq(y), ALU.mult)
                                own.wait_own()
                                w = [vcol("conv_w", 12 * l + 4 * c + p) for c in range(3)]
                                ts(seq(y), conv_in[:, 0:nseq, 0:TOK], w[0], ALU.mult)
                                own.wait_own()
                                stt(seq(y), conv_in[:, 0:nseq, 1:TOK + 1], w[1], seq(y), ALU.mult, ALU.add)
                                own.wait_own()
                                return stt_i(seq(y), conv_in[:, 0:nseq, 2:TOK + 2], w[2], seq(y), ALU.mult, ALU.add)
                            if kind == "cb":
                                return dve.tensor_tensor(y, y, zt, ALU.mult)
                            if kind == "cg":
                                silu(zt)
                                tt(se[:, 0:t_y], se[:, 0:t_y], zt, ALU.mult)
                                own.wait_own()
                                return dve.tensor_tensor(y, y, se[:, 0:t_y], ALU.mult)
                            y = res[:, 4 * p + 3, ycols]
                            if kind == "pu":
                                return dve.tensor_copy(y, zt)
                            silu(zt)
                            tt(se[:, 0:t_y], se[:, 0:t_y], zt, ALU.mult)
                            dve.wait_ge(pool_mm, 4 * l + p + 1)
                            own.wait_own()
                            return stt_i(y, att[5][:, 0:t_y], vcol("pool_scale", 4 * l + p), se[:, 0:t_y],
                                         ALU.mult, ALU.mult)

                        def before():
                            if kind == "ag":
                                for t in range(n_tiles):
                                    dve.wait_ge(exp_done, tiles(l, h) + t + 1)
                                    own.inc_own(dve.reciprocal(inv[:, 2 * t:2 * t + 2], sums[:, 2 * t:2 * t + 2]))
                                    own.wait_own()
                                    tt(inv[:, 2 * t + 1:2 * t + 2], inv[:, 2 * t + 1:2 * t + 2], lam_col[l], ALU.mult)
                                    ts(probs(t, 0), probs(t, 0), inv[:, 2 * t:2 * t + 1], ALU.mult)
                                    own.wait_own()
                                    own.inc(stt_i(probs(t, 0), probs(t, 1), inv[:, 2 * t + 1:2 * t + 2], probs(t, 0),
                                                     ALU.mult, ALU.add), a_full, tiles(l, h) + t + 1)

                        def after():
                            if kind == "v":
                                for group in ((0,), (1,), (2, 3))[:n_tiles - 1 if l == 0 else 2]:
                                    dve.wait_ge(s_done, tiles(l, h) + group[-1] + 1)
                                    for t in group:
                                        for m in range(2):
                                            own.inc_own(dve.reduce_max(top[:, 2 * t + m:2 * t + m + 1], scores(t, m), axis=AX))
                                    own.wait_own()
                                    for t in group:
                                        own.inc(dve.tensor_scalar(top_s[:, 2 * t:2 * t + 2], top[:, 2 * t:2 * t + 2],
                                                                     -DIFF_SCALE, None, ALU.mult),
                                                   top_done, tiles(l, h) + t + 1)
                            elif kind in ("cc", "pg"):
                                dve.wait_ge(rs_full, hh + 1)
                                for t in range(n_tiles):
                                    last = dve.tensor_scalar(o_sb[:, P * t:P * (t + 1)], att[3][:, P * t:P * (t + 1)],
                                                             o_rs[:, t:t + 1], None, ALU.mult)
                                own.inc(last, o_full, hh + 1)
                            elif kind in ("pu", "cb"):
                                dve.wait_ge(ot_done, hh + 1)
                                y = res[:, 4 * p + half, ycols]
                                tt(y, att[4][:, 0:t_y], y, ALU.mult)
                        slot(unit, epilogue, before, after)
                        if l == 0:
                            slot(unit.ahead(1), modulation(2 * KT + 14 * i + j // 2))
                    own.leave_loop(4 if l == 0 else 2)
                announce(y_all, l + 1)

            def residual(l, k, b, loaded):
                def epilogue(zz):
                    if l == 0:
                        dve.wait_ge(xres_in[b], 16 * loaded)
                        for s in range(2):
                            cols = slice(TOK * s, TOK * (s + 1))
                            ts(zz[:, cols], zz[:, cols], mod[:, 2 * KT + k, s:s + 1], ALU.mult)
                        own.wait_own()
                        return stt_i(res[:, k, :], x_res[b], ALPHA, zz, ALU.mult, ALU.add)
                    tt(zz[:, 0:TOK], zz[:, 0:TOK], zz[:, TOK:WIDE], ALU.add)
                    r = res[:, k, 0:TOK]
                    ts(r, r, vcol("ln_g", k), ALU.mult, vcol("ln_b", k), ALU.add)
                    own.wait_own()
                    return stt_i(r, zz[:, 0:TOK], mod[:, NMOD + 2 * KT + k, 0:1], r, ALU.mult, ALU.add)
                return epilogue

            def centre(l, k):
                t = WIDE if l == 0 else TOK
                own.wait_own()
                own.inc(stt_i(res[:, k, 0:t], att[0][:, 0:t], -float(KT), res[:, k, 0:t], ALU.mult, ALU.add),
                        cen_done, 16 * l + k + 1)
                own.wait_own()
                tt(total[:, 0:t], total[:, 0:t], res[:, k, 0:t], ALU.add)

            def add_square(l, k, b):
                t = WIDE if l == 0 else TOK
                dve.wait_ge(csq_full, 16 * l + k + 1)
                own.wait_own()
                own.inc(dve.tensor_tensor(total_sq[:, 0:t], total_sq[:, 0:t], squared[b][:, 0:t], ALU.add),
                        csq_used, 16 * l + k + 1)

            def clear_sums():
                for a in (total, total_sq):
                    own.inc_own(dve.memset(a, 0.0))

            def layer_out(l, begin, turns, k0, mods, steps):
                with dve.Fori(0, turns) as i:
                    own.enter_loop(i, steps)
                    for j in range(4):
                        unit = Unit(begin, i, 4, j)
                        if mods and j % 2:
                            slot(unit, modulation(LAYERS * NMOD - 6 + 2 * i + j // 2))
                            continue
                        n = j // 2 if mods else j
                        k = k0 + (2 * i if mods else 4 * i) + n
                        loaded = k0 // 2 + (i if mods else 2 * i + n // 2) + 1

                        def before():
                            add_square(l, k - 2, n % 2)

                        def after():
                            centre(l, k)
                        slot(unit, residual(l, k, n % 2, loaded), before, after)
                    own.leave_loop(turns)

            def add(k):
                def epilogue(zz):
                    tt(zz[:, 0:TOK], zz[:, 0:TOK], zz[:, TOK:WIDE], ALU.add)
                    own.wait_own()
                    r = res[:, k, 0:TOK]
                    return dve.tensor_tensor(r, r, zz[:, 0:TOK], ALU.add)
                return epilogue

            def add_down(k):
                def epilogue(zz):
                    zt = zz[:, 0:TOK]
                    tt(zt, zt, zz[:, TOK:WIDE], ALU.add)
                    own.wait_own()
                    tt(zt, zt, rms_mlp2, ALU.mult)
                    own.wait_own()
                    return dve.tensor_tensor(res[:, k, 0:TOK], res[:, k, 0:TOK], zt, ALU.add)
                return epilogue

            def finish_rsqrt(t, eps, n, variance=att[1], target=rstd):
                dve.wait_ge(lnx_done, n + 1)
                tt(newton[:, 0:t], rstd[:, 0:t], rstd[:, 0:t], ALU.mult)
                own.wait_own()
                stt(newton[:, 0:t], variance[:, 0:t], eps, newton[:, 0:t], ALU.add, ALU.mult)
                own.wait_own()
                ts(newton[:, 0:t], newton[:, 0:t], -0.5, ALU.mult, 1.5, ALU.add)
                own.wait_own()
                tt(target[:, 0:t], rstd[:, 0:t], newton[:, 0:t], ALU.mult)
                own.wait_own()

            def norm(l, t):
                add_square(l, KT - 2, 0)
                add_square(l, KT - 1, 1)
                announce(sum_full, l + 1)
                dve.wait_ge(mu_done, l + 1)
                own.inc(dve.tensor_copy(mean_sb[:, 0:t], att[2][:, 0:t]), mean_full, l + 1)
                own.wait_own()
                variance = a_t[:, 1, :]
                stt(variance[:, 0:t], mean_sb[:, 0:t], -1.0, mean_sb[:, 0:t], ALU.mult, ALU.mult)
                own.wait_own()
                own.inc(dve.tensor_tensor(variance[:, 0:t], variance[:, 0:t], att[1][:, 0:t], ALU.add), var_full, l + 1)
                for k in range(4):
                    tt(res[:, k, 0:t], res[:, k, 0:t], mean_sb[:, 0:t], ALU.subtract)
                finish_rsqrt(t, LN_EPS, l, variance)

                def rest(k, q, b):
                    if l == 0:
                        rest_x(2, k, h_buffer(l, q, b), x, WIDE)
                    else:
                        rest_x(4, k, h_buffer(l, q, b), xs, TOK)

                def two_tiles(pair, q, first=False):
                    k = 2 * pair
                    for b in range(2):
                        r = res[:, k + b, 0:t]
                        own.inc(dve.tensor_tensor(r, r, rstd[:, 0:t], ALU.mult), scaled, 16 * l + k + b + 1)
                    if l == 1:
                        own.wait_own()
                        for b in range(2):
                            r = res[:, k + b, 0:t]
                            ts(r, r, vcol("ln_g", KT + k + b), ALU.mult, vcol("ln_b", KT + k + b), ALU.add)
                    if not first:
                        for b in range(2):
                            rest(k - 2 + b, 1 - q, b)
                    own.wait_own()
                    if l == 0:
                        for s in range(2):
                            cols = slice(TOK * s, TOK * (s + 1))
                            last = dve.tensor_scalar(h_buffer(l, q, 1)[:, cols], res[:, k + 1, cols],
                                                     mod[:, NMOD + KT + k + 1, s:s + 1], mod[:, NMOD + k + 1, s:s + 1],
                                                     ALU.mult, ALU.add)
                        own.inc(last, odd_full, pair + 1)
                    else:
                        for b in range(2):
                            own.inc(dve.tensor_scalar(h_buffer(l, q, b), res[:, k + b, 0:TOK],
                                                      vcol("norm_mix_g", k + b), None, ALU.mult), h_full, 16 + k + b + 1)

                two_tiles(0, 0, first=True)
                two_tiles(1, 1)
                with dve.Fori(0, KT // 4 - 1) as i:
                    own.enter_loop(i, 0 if l == 0 else 4)
                    for q in range(2):
                        dve.wait_ge(minus_mean, 12 * l + 4 * i + 2 * q + 2)
                        two_tiles(2 * i + 2 + q, q)
                    own.leave_loop(KT // 4 - 1)
                for b in range(2):
                    rest(KT - 2 + b, 1, b)

            def fold_affine():
                gain, bias = (vec[:, VEC_COLS[v]:VEC_COLS[v] + KT] for v in ("ln_g", "ln_b"))
                own.wait_own()
                for s in range(2):
                    shift, scale = (mod[:, NMOD + c * KT:NMOD + (c + 1) * KT, s] for c in range(2))
                    tt(cond_e[:, :, s], scale, bias, ALU.mult)
                    own.wait_own()
                    tt(shift, shift, cond_e[:, :, s], ALU.add)
                    tt(scale, scale, gain, ALU.mult)
                own.wait_own()
                ts(gain, gain, ALPHA, ALU.mult)
                ts(bias, bias, ALPHA, ALU.mult)

            layer_in(0, STEPS["in0"])
            split_y(1, x, slice(0, WIDE))
            dve.wait_ge(o_full, HEADS)
            clear_sums()
            for j in range(4):
                unit = Unit(U_OUT0, 0, 4, j)
                if j % 2:
                    slot(unit, modulation(LAYERS * NMOD - 8 + j // 2))
                else:
                    slot(unit, residual(0, j // 2, j // 2, 1))
            dve.wait_ge(pivot_done, 1)
            centre(0, 0)
            centre(0, 1)
            layer_out(0, U_OUT0 + 4, 3, 2, True, STEPS["out0a"])
            fold_affine()
            layer_out(0, U_OUT0 + 16, 2, 8, False, STEPS["out0b"])
            norm(0, WIDE)
            layer_in(1, STEPS["in1"])
            split_y(3, x, slice(TOK, WIDE))
            clear_sums()
            for j in range(4):
                def before():
                    if j == 2:
                        dve.wait_ge(pivot_done, 2)
                        centre(1, 0)
                        centre(1, 1)

                def after():
                    if j >= 2:
                        centre(1, j)
                    if j == 3:
                        add_square(1, 0, 0)
                        add_square(1, 1, 1)
                slot(Unit(U_OUT1, 0, 4, j), residual(1, j, j % 2, None), before, after)
            layer_out(1, U_OUT1 + 4, 3, 4, False, STEPS["out1"])
            dve.wait_ge(f_hi, 1)
            own.inc(dve.tensor_tensor(wf_lo[:], wf_raw[:], wf_hi[:].bitcast(F32), ALU.subtract), f_lo, 1)
            norm(1, TOK)

            finish_rsqrt(TOK, RMS_EPS, 2, target=rms_mix)

            dve.wait_ge(f_mm, 1)
            own.inc_own(dve.tensor_copy(gate_rows, att[3][0:HEADS, TOK:WIDE]))
            own.wait_own()
            tt(log_rows, att[3][0:HEADS, 0:TOK], gate_rows, ALU.add)
            own.wait_own()
            tt(log_rows, log_rows, rms_mix[0:HEADS, :], ALU.mult)
            own.wait_own()
            ts(log_rows, log_rows, vcol("b_forget", 0)[0:HEADS, :], ALU.add)
            own.wait_own()
            ts(gate_rows, log_rows, -1.0, ALU.mult)
            own.wait_own()
            own.inc(dve.tensor_tensor(gate_rows, gate_rows, log_rows, ALU.max), f_in, 1)
            own.wait_own()
            ts(log_rows, log_rows, 0.0, ALU.min)
            dve.wait_ge(f_exp, 1)
            own.wait_own()
            own.inc(dve.tensor_tensor(log_rows, log_rows, gate_rows, ALU.subtract), f_full, 1)
            ts(vec[:, VEC_COLS["slope"]:VEC_COLS["slope"] + HEADS], vec[:, VEC_COLS["slope"]:VEC_COLS["slope"] + HEADS],
               1.0 / HEAD_SCALE, ALU.mult)

            def take_output(p, c):
                dve.wait_ge(o_done, HEADS1 + 2 * p + c + 1)
                own.inc_own(dve.tensor_copy(res[:, HEADS * c + p, TOK:WIDE], att[3][:, 0:TOK]))

            with dve.Fori(0, 4) as i:
                own.enter_loop(i, STEPS["in2"])
                for half in range(2):
                    p = 2 * i + half
                    for s, kind in enumerate(IN2_SLOTS):
                        unit = Unit(U_IN2, i, 20, 10 * half + s)
                        gate = 32 + 4 * p + s - 6 if s >= 6 else None
                        c = int(kind[1] == "b")

                        def epilogue(zz):
                            zt = zz[:, 0:TOK]
                            cols = slice(TOK * c, TOK * (c + 1))
                            tt(zt, zt, zz[:, TOK:WIDE], ALU.add)
                            own.wait_own()
                            if kind[0] in "qkv":
                                target = {"q": q_t, "k": k_t, "v": v_t}[kind[0]]
                                return dve.tensor_tensor(target[:, cols], zt, rms_mix, ALU.mult)
                            own.inc(dve.tensor_tensor(zt, zt, rms_mix, ALU.mult), z_sum, gate - 16 + 1)
                            dve.wait_ge(se_full, gate + 1)
                            ts(se[:, 0:TOK], se[:, 0:TOK], 1.0, ALU.add)
                            own.wait_own()
                            return dve.reciprocal(gates[:, KT * c + 2 * p + s % 2, :], se[:, 0:TOK])

                        def before():
                            if kind == "va":
                                dve.wait_ge(lf_done, p + 1)
                                own.inc_own(dve.tensor_copy(log_f[:], att[4][:, TOK:TOK + 2]))
                                own.wait_own()
                                for t in range(2):
                                    last = dve.tensor_scalar(log_b[:, t, :], table_sb[:, 4, P:2 * P],
                                                             log_f[:, t:t + 1], -1.0 / HEAD_SCALE, ALU.mult, ALU.mult)
                                own.inc(last, lb_full, p + 1)
                            elif kind in ("qb", "ga0"):
                                c2 = int(kind == "ga0")
                                dve.wait_ge(exp_done, TILES1 + 2 * p + c2 + 1)
                                own.inc_own(dve.reciprocal(inv[:, 2 * c2:2 * c2 + 2], sums[:, 2 * c2:2 * c2 + 2]))
                                own.wait_own()
                                for t in range(2):
                                    w = work[:, 2 * c2 + t, 0:P * (t + 1)]
                                    last = dve.tensor_scalar(w, w, inv[:, 2 * c2 + t:2 * c2 + t + 1], None, ALU.mult)
                                own.inc(last, a_full, TILES1 + 2 * p + c2 + 1)
                                if c2:
                                    take_output(p, 0)
                            elif kind == "kb":
                                dve.wait_ge(f_cum, p + 1)
                                ts(cum_f[:], att[4][:, TOK + 2:TOK + 4], 1.0 / HEAD_SCALE, ALU.mult)

                        def after():
                            if kind in ("va", "vb"):
                                count = TILES1 + 2 * p + c
                                dve.wait_ge(s_done, count + 1)
                                dve.wait_ge(o_done, HEADS1 + 2 * p)
                                for t in range(2):
                                    keys = P * (t + 1)
                                    w = work[:, 2 * c + t, 0:keys]
                                    sc = att[c][:, TOK * t:TOK * t + keys]
                                    if c == 0:
                                        stt(w, table_sb[:, t, 0:keys], vcol("slope", p), sc, ALU.mult, ALU.add)
                                    else:
                                        stt(w, sc, cum_f[:, t:t + 1], table_sb[:, 2 + t, 0:keys], ALU.add, ALU.add)
                                own.wait_own()
                                for t in range(2):
                                    own.inc_own(dve.reduce_max(top[:, 2 * c + t:2 * c + t + 1],
                                                            work[:, 2 * c + t, 0:P * (t + 1)], axis=AX))
                                own.wait_own()
                                own.inc(dve.tensor_scalar(top_s[:, 2 * c:2 * c + 2], top[:, 2 * c:2 * c + 2],
                                                             -HEAD_SCALE, None, ALU.mult), top_done, count + 1)
                            elif kind == "gb0":
                                take_output(p, 1)
                        slot(unit, epilogue, before, after)
                own.leave_loop(4)
            split_y(5, xs, slice(TOK, WIDE))

            with dve.Fori(0, 4) as i:
                own.enter_loop(i, STEPS["proj"])
                for j in range(4):
                    unit = Unit(U_PROJ, i, 4, j)
                    k = 4 * i + j

                    def epilogue(zz):
                        zb = z_b[:, j % 2, :]
                        tt(zz[:, 0:TOK], zz[:, 0:TOK], zz[:, TOK:WIDE], ALU.add)
                        tt(zb[:, 0:TOK], zb[:, 0:TOK], zb[:, TOK:WIDE], ALU.add)
                        own.wait_own()
                        tt(zz[:, 0:TOK], zz[:, 0:TOK], gates[:, k, :], ALU.mult)
                        tt(zb[:, 0:TOK], zb[:, 0:TOK], gates[:, KT + k, :], ALU.mult)
                        own.wait_own()
                        return dve.tensor_tensor(res[:, k, TOK:WIDE], zz[:, 0:TOK], zb[:, 0:TOK], ALU.add)
                    slot(unit, epilogue)
                own.leave_loop(4)
            announce(y_all, 3)
            split_y(6, xs, slice(TOK, WIDE))
            own.inc_own(dve.memset(total_sq, 0.0))
            with dve.Fori(0, 4) as i:
                own.enter_loop(i, STEPS["out2"])
                for j in range(4):
                    k = 4 * i + j

                    def after():
                        own.wait_own()
                        h = h_tmp[j % 2][:, 0:TOK]
                        own.inc(dve.tensor_scalar(h, res[:, k, 0:TOK], vcol("norm_mlp_g", k), None, ALU.mult),
                                h_full, 32 + k + 1)
                        rest_x(7, k, h, mlp_x, TOK)
                        add_square(2, k, j % 2)
                    slot(Unit(U_OUT2, i, 4, j), add(k), after=after)
                own.leave_loop(4)
            finish_rsqrt(TOK, RMS_EPS, 3)
            tt(rms_mlp2, rstd[:, 0:TOK], rstd[:, 0:TOK], ALU.mult)
            own.wait_own()

            for c in range(4):
                with dve.Fori(0, 4) as i:
                    own.enter_loop(i, STEPS["up"])
                    for j in range(4):
                        k = 4 * i + j
                        unit = Unit(U_MLP + 32 * c, i, 4, j)

                        def epilogue(zz):
                            tt(zz[:, 0:TOK], zz[:, 0:TOK], zz[:, TOK:WIDE], ALU.add)
                            own.wait_own()
                            stt(h_tmp[0][:, 0:TOK], zz[:, 0:TOK], 0.0, zz[:, 0:TOK], ALU.max, ALU.mult)
                            own.wait_own()
                            own.inc(dve.memset(tiny[:, 62:63], 0.0), h_full, 48 + 16 * c + k + 1)
                            return dve.memset(tiny[:, 61:62], 0.0)

                        def after():
                            rest_x(8 + c, k, h_tmp[0][:, 0:TOK], hidden, TOK)
                        slot(unit, epilogue, after=after)
                    own.leave_loop(4)
                down = U_MLP + 32 * c + 16
                if c < 3:
                    with dve.Fori(0, 4) as i:
                        own.enter_loop(i, STEPS["down"])
                        for j in range(4):
                            slot(Unit(down, i, 4, j), add_down(4 * i + j))
                        own.leave_loop(4)
                    continue

                def finish(k, b):
                    own.wait_own()
                    ts(res[:, k, TOK:WIDE], res[:, k, 0:TOK], vcol("norm_final_g", k), ALU.mult)
                    add_square(3, k, b)

                own.inc_own(dve.memset(total_sq, 0.0))
                with dve.Fori(0, 3) as i:
                    own.enter_loop(i, STEPS["last_down"])
                    for j in range(4):
                        slot(Unit(down, i, 4, j), add_down(4 * i + j), after=lambda: finish(4 * i + j, j % 2))
                    own.leave_loop(3)
                for j in range(4):
                    slot(Unit(UNITS - 4, 0, 4, j), add_down(12 + j), after=lambda: finish(12 + j, j % 2),
                         last=j >= 2)
            finish_rsqrt(TOK, RMS_EPS, 4)
            with dve.Fori(0, KT // 2) as i:
                own.enter_loop(i, 0)
                for b in range(2):
                    k = 2 * i + b
                    r = res[:, k, TOK:WIDE]
                    own.inc(dve.tensor_tensor(r, r, rstd[:, 0:TOK], ALU.mult), out_full, k + 1)
                own.leave_loop(KT // 2)

        @block.tensor
        def _(pe):
            def product(unit, mode, phase=None, operand=None):
                bank = gemm_bank[unit.slot % 2]
                for g in range(2):
                    pe.wait_ge(lo_done, 2 * unit.number + g + 1)
                    if g == 0 and (unit.exact[3] >= 2 or unit.exact[0] > 0 or not isinstance(unit.exact[1], int)):
                        pe.wait_ge(z_full, unit.number - 1)
                    n = 2 * (unit.slot % 2) + g
                    for kk in range(KT // 2):
                        k = 8 * g + kk
                        if phase is not None and kk % 2 == 0:
                            pe.wait_ge(x_full, 16 * phase + k + 2)
                        hi = w_hi[:, n, P * kk:P * (kk + 1)]
                        lo = w_lo[:, n, P * kk:P * (kk + 1)]
                        first, last = k == 0, k == KT - 1
                        if mode == "mod":
                            pe.matmul(bank[0:SQUARE, 0:P], cond_x[:, k, :], hi, start=first, stop=False)
                            ins = pe.matmul(bank[0:SQUARE, 0:P], cond_x[:, k, :], lo, start=False, stop=last)
                        elif mode == "wide":
                            pe.matmul(bank[:, :], hi, operand[:, k, 0, :], start=first, stop=False)
                            pe.matmul(bank[:, :], hi, operand[:, k, 1, :], start=False, stop=False)
                            ins = pe.matmul(bank[:, :], lo, operand[:, k, 0, :], start=False, stop=last)
                        elif mode == "pair":
                            b = bank if g == 0 else att[unit.slot % 2]
                            first, last = kk == 0, kk == KT // 2 - 1
                            pe.matmul(b[:, :].rearrange("p (a t) -> p a t", a=2), hi, operand[:, k, :, 0:TOK],
                                      start=first, stop=False)
                            ins = pe.matmul(b[:, 0:TOK], lo, operand[:, k, 0, 0:TOK], start=False, stop=last)
                        else:
                            pe.matmul(bank[:, :].rearrange("p (a t) -> p a t", a=2), hi, operand[:, k, :, 0:TOK],
                                      start=first, stop=False)
                            ins = pe.matmul(bank[:, 0:TOK], lo, operand[:, k, 0, 0:TOK], start=False, stop=last)
                    ins.then_inc(half_used, 1)

            pe.wait_ge(cond_full, 1)
            for j in range(4):
                product(Unit(0, 0, 4, j), "mod")
            with pe.Fori(0, U_IN0 // 4 - 1) as i:
                for j in range(4):
                    product(Unit(4, i, 4, j), "mod")
            pe.wait_ge(const_in, 16 * 4)

            def layer_in(l):
                n_tiles = 4 if l == 0 else 2
                with pe.Fori(0, 4 if l == 0 else 2) as i:
                    for j, kind, pair, half, wide in in_slots(l):
                        p = i if l == 0 else 2 * i + pair
                        h = 2 * p + half
                        hh = 8 * l + h
                        unit = Unit(U_IN[l], i, 28, j)
                        product(unit, "wide" if wide else "narrow", 0 if l == 0 else 2, x)
                        if kind == "cg":
                            pe.wait_ge(pool_w_in, 64 * l + 16 * p + 16)
                            pe.wait_ge(pool_d, 4 * l + p + 1)
                            pe.wait_ge(v_full, hh + 1)
                            ycols = slice(0, WIDE) if l == 0 else slice(TOK, WIDE)
                            pe.matmul(att[5][:, 0:ycols.stop - ycols.start], pool_sb[:, :],
                                      res[:, 4 * p + 3, ycols], start=True, stop=True).then_inc(pool_mm, 1)
                        if kind == "v":
                            pe.wait_ge(z_used, unit.number if l == 1 else unit.number - 1)
                            for t in range(n_tiles):
                                keys = slice(0, WIDE) if t < 2 else slice(TOK, WIDE)
                                for m in range(2):
                                    rows = slice(QK * m, QK * (m + 1))
                                    o = att[2 * t + m][:, :] if t < 2 else att[4 + m][:, TOK * (t - 2):TOK * (t - 1)]
                                    ins = pe.matmul(o, q_t[rows, P * t:P * (t + 1)], k_t[rows, keys],
                                                    start=True, stop=True)
                                ins.then_inc(s_done, 1)
                        elif kind == "ag":
                            if l == 0:
                                pe.wait_ge(exp_done, tiles(l, h) + 4)
                            pe.wait_ge(z_used, unit.number if l == 1 else unit.number - 1)
                            for t in range(4):
                                ins = pe.transpose(att[5][:, P * t:P * (t + 1)], v_t[:, P * t:P * (t + 1)], ident[:])
                            ins.then_inc(vt_done, 1)
                        elif kind in ("cu", "cg"):
                            for t in range(2):
                                pe.wait_ge(a_full, tiles(l, h) + t + 1)
                                for c in range(4):
                                    ins = pe.transpose(att[t][:, P * c:P * (c + 1)], probs(t, 0)[:, P * c:P * (c + 1)],
                                                       ident[:])
                                ins.then_inc(t_done, 1)
                            if l == 0:
                                pe.wait_ge(a_full, tiles(l, h) + 4)
                                for t in range(2, 4):
                                    for c in range(2):
                                        n = 2 * (t - 2) + c
                                        ins = pe.transpose(att[2][:, P * n:P * (n + 1)], probs(t, 0)[:, P * c:P * (c + 1)],
                                                           ident[:])
                                ins.then_inc(t_done, 1)
                        elif kind in ("cc", "pg"):
                            pe.wait_ge(v_full, hh + 1)
                            pe.wait_ge(at_full, t_banks(l, h) + (3 if l == 0 else 2))
                            for t in range(n_tiles):
                                o = att[3][:, P * t:P * (t + 1)]
                                n_keys = 4 if t < 2 else 2
                                for c in range(n_keys):
                                    a = a_t[:, t, P * c:P * (c + 1)] if t < 2 else \
                                        a_t[:, 2, P * (2 * (t - 2) + c):P * (2 * (t - 2) + c + 1)]
                                    ins = pe.matmul(o, a, v_tok[:, 4 - n_keys + c, :], start=c == 0, stop=c == n_keys - 1)
                            ins.then_inc(o_done, 1)
                        elif kind in ("pu", "cb"):
                            pe.wait_ge(o_full, hh + 1)
                            for t in range(n_tiles):
                                ins = pe.transpose(att[4][:, P * t:P * (t + 1)], o_sb[:, P * t:P * (t + 1)], ident[:])
                            ins.then_inc(ot_done, 1)
                        if l == 0:
                            product(unit.ahead(1), "mod")

            def plain(begin, turns, mode, phase, operand, mods=False):
                with pe.Fori(0, turns) as i:
                    for j in range(4):
                        if mods and j % 2:
                            product(Unit(begin, i, 4, j), "mod")
                        else:
                            product(Unit(begin, i, 4, j), mode, phase, operand)

            def mean_square(n):
                pe.wait_ge(csq_used, 16 * n + 16)
                pe.matmul(att[1][:, 0:TOK], mean_w[:], total_sq[:, 0:TOK], start=True, stop=True).then_inc(ms_done, 1)

            def pivot(l, t):
                pe.wait_ge(z_used, [U_OUT0, U_OUT1][l] + 1)
                pe.matmul(att[0][:, 0:t], mean_w[:], res[:, 0, 0:t], start=True, stop=True).then_inc(pivot_done, 1)

            def means(l, t):
                pe.wait_ge(sum_full, l + 1)
                ins = pe.matmul(att[2][:, 0:t], mean_w[:], total[:, 0:t], start=True, stop=True)
                if l == 1:
                    ins.then_inc(sq_used, 1)
                pe.matmul(att[1][:, 0:t], mean_w[:], total_sq[:, 0:t], start=True, stop=True).then_inc(mu_done, 1)

            layer_in(0)
            for j in range(4):
                product(Unit(U_OUT0, 0, 4, j), "mod" if j % 2 else "wide", None if j % 2 else 1, x)
            pivot(0, WIDE)
            plain(U_OUT0 + 4, 3, "wide", 1, x, mods=True)
            plain(U_OUT0 + 16, 2, "wide", 1, x)
            means(0, WIDE)
            layer_in(1)
            for j in range(4):
                product(Unit(U_OUT1, 0, 4, j), "narrow", 3, x)
                if j == 1:
                    pivot(1, TOK)
            plain(U_OUT1 + 4, 3, "narrow", 3, x)
            means(1, TOK)
            pe.wait_ge(f_lo, 1)
            for k in range(KT):
                pe.wait_ge(x_full, 16 * 4 + k + 1)
                pe.matmul(att[3][0:HEADS, :].rearrange("p (a t) -> p a t", a=2), wf_hi[:, k, :], xs[:, k, :, :],
                          start=k == 0, stop=False)
                ins = pe.matmul(att[3][0:HEADS, 0:TOK], wf_lo[:, k, :], xs[:, k, 0, :], start=False, stop=k == KT - 1)
                if k == KT - 1:
                    ins.then_inc(f_mm, 1)
                pe.wait_ge(sq_full, k + 1)
                pe.matmul(att[1][:, 0:TOK], mean_w[:], sq[k % 2][:, 0:TOK], start=k == 0, stop=k == KT - 1)\
                  .then_inc(sq_used, 1)

            with pe.Fori(0, 4) as i:
                for half in range(2):
                    p = 2 * i + half
                    for s, kind in enumerate(IN2_SLOTS):
                        unit = Unit(U_IN2, i, 20, 10 * half + s)
                        product(unit, "narrow", 4, xs)
                        if kind == "ka":
                            pe.wait_ge(f_full, 1)
                            pe.wait_ge(z_used, unit.number)
                            for t in range(2):
                                ins = pe.matmul(att[4][:, TOK + t:TOK + t + 1], log_rows[:, P * t:P * (t + 1)],
                                                ident[0:HEADS, bass.ds(p, 1)], start=True, stop=True)
                            ins.then_inc(lf_done, 1)
                        c = int(kind == "vb")
                        if kind in ("va", "vb"):
                            pe.wait_ge(z_used, unit.number)
                            if c == 1:
                                pe.wait_ge(lb_full, p + 1)
                            for t in range(2):
                                keys = P * (t + 1)
                                o = att[c][:, TOK * t:TOK * t + keys]
                                q = q_t[:, TOK * c + P * t:TOK * c + P * (t + 1)]
                                ins = pe.matmul(o, q, k_t[:, TOK * c:TOK * c + keys], start=True, stop=c == 0)
                                if c == 1:
                                    ins = pe.matmul(o, log_b[:, 0, :], table_sb[:, 4, 0:keys], start=False, stop=t == 0)
                                    if t == 1:
                                        ins = pe.matmul(att[c][:, TOK + P:2 * TOK], log_b[:, 1, :], table_sb[:, 4, 0:P],
                                                        start=False, stop=True)
                            ins.then_inc(s_done, 1)
                        elif kind in ("qb", "ga0"):
                            c = int(kind == "ga0")
                            pe.wait_ge(z_used, unit.number)
                            for t in range(2):
                                a = TOK * c + P * t
                                ins = pe.transpose(att[5][:, P * t:P * (t + 1)], v_t[:, a:a + P], ident[:])
                            ins.then_inc(vt_done, 1)
                            if kind == "qb":
                                pe.wait_ge(lb_full, p + 1)
                                o = att[4][:, TOK + 2:TOK + 4]
                                pe.matmul(o[:, 0:1], table_sb[:, 4, 0:P], log_f[:, 0:1], start=True, stop=True)
                                pe.matmul(o[:, 1:2], table_sb[:, 4, P:2 * P], log_f[:, 0:1], start=True, stop=False)
                                pe.matmul(o[:, 1:2], table_sb[:, 4, 0:P], log_f[:, 1:2], start=False, stop=True)\
                                  .then_inc(f_cum, 1)
                        elif kind in ("kb", "ga1"):
                            c = int(kind == "ga1")
                            pe.wait_ge(a_full, TILES1 + 2 * p + c + 1)
                            for n, (t, kb) in enumerate(((0, 0), (1, 0), (1, 1))):
                                ins = pe.transpose(att[2][:, P * n:P * (n + 1)],
                                                   work[:, 2 * c + t, P * kb:P * (kb + 1)], ident[:])
                            ins.then_inc(t_done, 1)
                        if kind in ("vb", "gb0"):
                            c = int(kind == "gb0")
                            pe.wait_ge(v_full, HEADS1 + 2 * p + c + 1)
                            pe.wait_ge(at_full, TBANKS1 + 2 * p + c + 1)
                            pe.wait_ge(z_used, unit.number)
                            first, second = v_tok[:, 2 * c, :], v_tok[:, 2 * c + 1, :]
                            pe.matmul(att[3][:, 0:P], first, a_t[:, c, 0:P], start=True, stop=True)
                            pe.matmul(att[3][:, P:2 * P], first, a_t[:, c, P:2 * P], start=True, stop=False)
                            pe.matmul(att[3][:, P:2 * P], second, a_t[:, c, 2 * P:3 * P],
                                      start=False, stop=True).then_inc(o_done, 1)

            plain(U_PROJ, 4, "pair", 5, xs)
            plain(U_OUT2, 4, "narrow", 6, xs)
            for j in range(4):
                product(Unit(U_MLP, 0, 4, j), "narrow", 7, mlp_x)
                if j == 0:
                    mean_square(2)
            plain(U_MLP + 4, 3, "narrow", 7, mlp_x)
            for c in range(4):
                if c:
                    plain(U_MLP + 32 * c, 4, "narrow", 7, mlp_x)
                plain(U_MLP + 32 * c + 16, 4, "narrow", 8 + c, hidden)
            mean_square(3)


STEPS = {"mod": 4, "in0": 85, "out0a": 8, "out0b": 12, "in1": 110, "out1": 12, "in2": 56, "proj": 16, "out2": 4, "down": 8, "last_down": 12, "up": 8}


def units_of(w):
    n = w.shape[1] // P
    return w.reshape(KT, P, n, P).transpose(2, 1, 0, 3).reshape(n, P, UNIT)


def columns(v):
    return np.ascontiguousarray(v).reshape(-1, P).T


def in_order(w):
    u = units_of(w)
    cu, cb, cc, cg, q, k, v, ag, pu, pg = np.split(np.arange(56), [4, 8, 12, 16, 24, 32, 40, 48, 52])
    where = {"cu": cu, "cb": cb, "cc": cc, "cg": cg, "pu": pu, "pg": pg}
    heads = {"q": q, "k": k, "v": v, "ag": ag}
    order = [heads[kind][2 * pair + half] if kind in heads else where[kind][pair]
             for pair in range(4) for kind, half in IN_SLOTS]
    return u[np.array(order)]


def mixer_rows(w):
    order = [tile for p in range(4) for tile in (4 + 2 * p, 5 + 2 * p, p, 12 + p)]
    return w.reshape(KT, P, -1)[np.array(order)].reshape(w.shape)


def weight_stream(a):
    shift, scale = units_of(a["w_mod"][0][:, :D]), units_of(a["w_mod"][0][:, D:2 * D])
    parts = [np.stack([shift, scale], 1).reshape(-1, P, UNIT)]
    mods = np.concatenate([units_of(a["w_mod"][0][:, 2 * D:]), units_of(a["w_mod"][1])])
    u = in_order(a["w_in"][0])
    parts.append(np.stack([u, mods[:56]], 1).reshape(-1, P, UNIT))
    u = units_of(mixer_rows(a["w_out"][0]))
    parts.append(np.stack([u[:8], mods[56:]], 1).reshape(-1, P, UNIT))
    parts += [u[8:], in_order(a["w_in"][1]), units_of(mixer_rows(a["w_out"][1]))]
    w = a["w_in_2"]
    u = units_of(np.concatenate([w[:, :6144], w[:, 6152:]], 1))
    starts = {"qa": 0, "ka": 8, "va": 16, "qb": 24, "kb": 32, "vb": 40}
    order = []
    for p in range(HEADS):
        order += [starts[s] + p for s in IN2_SLOTS[:6]]
        order += [48 + 2 * p, 48 + 2 * p + 1, 64 + 2 * p, 64 + 2 * p + 1]
    parts.append(u[np.array(order)])
    parts.append(units_of(np.concatenate([a["w_proj_a_2"], a["w_proj_b_2"]], 0)))
    parts.append(units_of(a["w_out_2"]))
    for c in range(4):
        parts.append(units_of(a["w_up_2"][:, D * c:D * (c + 1)]))
        parts.append(units_of(a["w_down_2"][D * c:D * (c + 1)]))
    return np.concatenate(parts)


def shape_tables():
    n = QK // 4
    inv = 10000.0 ** (-np.arange(n, dtype=np.float32) / n)
    t = np.arange(TOK)
    by_row, by_col = (t // 64)[None, :] * inv[:, None], (t % 64)[None, :] * inv[:, None]
    angle = np.concatenate([by_row, by_row, by_col, by_col] * 2).astype(np.float32)
    sign = np.where(np.arange(P) % 32 < 16, -1.0, 1.0)[:, None]
    rope = np.stack([np.cos(angle), np.sin(angle) * sign], 1).astype(np.float32)
    squares = np.stack([np.eye(P), np.full((P, P), 1.0 / D)], 1).astype(np.float32)
    q, k = np.arange(P)[:, None], np.arange(TOK)[None, :]
    tables = np.zeros((P, 5, TOK), np.float32)
    for b in range(2):
        far = (q + P * b) - k
        tables[:, b] = np.where(far >= 0, -far, MASKED)
        tables[:, 2 + b] = np.where(far >= 0, 0.0, MASKED)
    tables[:, 4] = q <= k
    edge = np.zeros((4, 16), np.float32)
    for g, w in enumerate(WINDOWS):
        for e in range(16):
            tok = e if e < 8 else TOK - 16 + e
            edge[g, e] = w / (min(tok + w - w // 2, TOK) - max(tok - w // 2, 0))
    slope = 2.0 ** (-8.0 * np.arange(1, HEADS + 1) / HEADS)
    return rope, squares, tables, edge.reshape(-1), slope.astype(np.float32)


def kernel(**inputs):
    import concourse.bacc as bacc
    from concourse.bass_utils import run_bass_kernel_spmd

    a = {k: np.asarray(v) for k, v in inputs.items()}
    rope, squares, tables, edge, slope = shape_tables()

    def spread(v):
        return np.broadcast_to(v.reshape(1, -1), (P, v.size))

    vec = [columns(a["b_mod"]),
           columns(a["conv_w"]), a["subln_g"].T, columns(a["pool_scale"]), columns(a["ln_g"]), columns(a["ln_b"]),
           columns(a["norm_mix_g_2"]), columns(a["norm_mlp_g_2"]), columns(a["norm_final_g_2"]),
           np.pad(a["b_forget_2"], (0, P - HEADS))[:, None], spread(slope), spread(edge)]
    lam = np.stack([a["lam_q1"], a["lam_k1"], a["lam_q2"], a["lam_k2"]], 1)
    both = np.concatenate([a["x"][0], a["ctx"][0]], 0)
    arrays = {
        "stream": weight_stream(a),
        "tokens": both.T.reshape(KT, P, WIDE).transpose(1, 0, 2),
        "cond": np.stack([a["c"][0], a["c_ctx"]], 0).reshape(2, KT, P).transpose(2, 1, 0),
        "vectors": np.concatenate(vec, 1),
        "lam_in": spread(lam),
        "pool_w": a["pool_w"].reshape(LAYERS * 4, P, P),
        "w_forget": a["w_in_2"][:, 6144:6152].reshape(KT, P, HEADS).transpose(1, 0, 2),
        "rope": rope, "squares": squares, "tables": tables,
    }
    arrays = {k: np.ascontiguousarray(v) for k, v in arrays.items()}
    nc = bacc.Bacc("TRN2", target_bir_lowering=False, num_devices=1)
    args = [nc.dram_tensor(k, v.shape, mybir.dt.from_np(v.dtype), kind="ExternalInput").ap()
            for k, v in arrays.items()]
    out = nc.dram_tensor("out", (P, KT, TOK), F32, kind="ExternalOutput").ap()
    two_blocks(nc, *args, out)
    r = run_bass_kernel_spmd(nc, [arrays], core_ids=[0])
    y = r.results[0]["out"]
    return np.ascontiguousarray(y.transpose(2, 1, 0)).reshape(1, TOK, D)
```
